# Optimizing a Trainium2 kernel written in Bass

```python
import jax, jax.numpy as jnp
from jax import lax
import numpy as np

D_MODEL = 1024
BATCH = 1
SEQ = 128
DEPTH = 2
DEC_BATCH = 1
DEC_SEQ = 512
PAST_LEN = 128

GRID_W = 64
BLOCK = 128
ROPE_BASE = 10000.0
EPS = 1e-6
N_Q_HEADS = 8
N_KV_HEADS = 2
HEAD_DIM = 64
ATT_Q = N_Q_HEADS * HEAD_DIM
ATT_KV = N_KV_HEADS * HEAD_DIM
N_RET_HEADS = 4
RET_DK = 128
RET_DV = 128
RET_W = N_RET_HEADS * RET_DK
N_MLP_GROUPS = 4
MLP_W = 512
MLP_GC = MLP_W // N_MLP_GROUPS
N_BRANCH = 3
IN_COLS = ATT_Q + 2 * ATT_KV + 4 * RET_W + 2 * MLP_W + N_BRANCH * D_MODEL
N_MOD = 6
N_EXPERTS = 16
N_EXPERT_GROUPS = 4
EXPERTS_PER_GROUP = N_EXPERTS // N_EXPERT_GROUPS
TOP_K = 2
EXPERT_FF = 512
MOE_BLOCK = 128

kernel_name = 'hybrid_diffusion_prefix_trunk_step'

def rms_norm(x, g):
    xf = x.astype(jnp.float32)
    y = xf * lax.rsqrt(jnp.mean(xf * xf, axis=-1, keepdims=True) + EPS)
    return (y * g.astype(jnp.float32)).astype(x.dtype)

def axial_rope(rows, dim):
    r = jnp.repeat(jnp.arange(rows, dtype=jnp.float32), GRID_W)
    col = jnp.tile(jnp.arange(GRID_W, dtype=jnp.float32), rows)
    half = dim // 2
    inv = ROPE_BASE ** (-jnp.arange(0, half, 2, dtype=jnp.float32) / half)
    ar = r[:, None] * inv
    ac = col[:, None] * inv
    ang = jnp.concatenate([ar, ar, ac, ac], axis=-1)
    return jnp.cos(ang), jnp.sin(ang)

def apply_rope(x, cos, sin):
    x1, x2, x3, x4 = jnp.split(x, 4, axis=-1)
    rot = jnp.concatenate([-x2, x1, -x4, x3], axis=-1)
    return (x * cos[:, None, :] + rot * sin[:, None, :]).astype(x.dtype)

def modulation(cond, w, b):
    m = jnp.einsum('bd,de->be', jax.nn.silu(cond), w) + b
    return [t[:, None, :] for t in jnp.split(m, N_MOD, axis=-1)]

def block_attention(q, k, v):
    B, Sq, Hq, dh = q.shape
    Hkv = k.shape[2]
    G = Hq // Hkv
    qb = q.reshape(B, Sq // BLOCK, BLOCK, Hkv, G, dh).transpose(1, 0, 2, 3, 4, 5)
    scale = dh ** -0.5

    def one_block(qi):
        s = jnp.einsum('bqhgd,bkhd->bhgqk', qi, k, preferred_element_type=jnp.float32) * scale
        p = jax.nn.softmax(s, axis=-1).astype(v.dtype)
        return jnp.einsum('bhgqk,bkhd->bqhgd', p, v)

    o = lax.map(one_block, qb)
    return o.transpose(1, 0, 2, 3, 4, 5).reshape(B, Sq, Hq * dh)

def retention_chunked(q, k, v, log_gamma, s0):
    B, S, H, dk = q.shape
    dv = v.shape[-1]
    N = S // BLOCK
    qc = q.astype(jnp.float32).reshape(B, N, BLOCK, H, dk)
    kc = k.astype(jnp.float32).reshape(B, N, BLOCK, H, dk)
    vc = v.astype(jnp.float32).reshape(B, N, BLOCK, H, dv)
    i = jnp.arange(BLOCK, dtype=jnp.float32)
    diff = i[:, None] - i[None, :]
    dmat = jnp.exp(jnp.where(diff[None] >= 0, diff[None] * log_gamma[:, None, None], -jnp.inf))
    inner = jnp.einsum('bnihd,bnjhd->bnhij', qc, kc) * dmat[None, None]
    o_inner = jnp.einsum('bnhij,bnjhe->bnihe', inner, vc)
    k_dec = kc * jnp.exp((BLOCK - 1 - i)[:, None] * log_gamma)[None, None, :, :, None]
    kv = jnp.einsum('bnjhd,bnjhe->nbhde', k_dec, vc)
    chunk_decay = jnp.exp(BLOCK * log_gamma)[None, :, None, None]

    def step(s, kv_n):
        return chunk_decay * s + kv_n, s

    s_end, s_start = lax.scan(step, s0.astype(jnp.float32), kv)
    q_dec = qc * jnp.exp((i + 1)[:, None] * log_gamma)[None, None, :, :, None]
    o_cross = jnp.einsum('bnihd,nbhde->bnihe', q_dec, s_start)
    return (o_inner + o_cross).reshape(B, S, H, dv), s_end

def bidir_retention(q, k, v, lg_f, lg_b, s0_f, s0_b):
    o_f, s_f = retention_chunked(q, k, v, lg_f, s0_f)
    o_b, s_b = retention_chunked(q[:, ::-1], k[:, ::-1], v[:, ::-1], lg_b, s0_b)
    return o_f + o_b[:, ::-1], s_f, s_b

def head_group_norm(o, g):
    mu = jnp.mean(o, axis=-1, keepdims=True)
    var = jnp.mean(jnp.square(o - mu), axis=-1, keepdims=True)
    y = (o - mu) * lax.rsqrt(var + EPS)
    return y.reshape(o.shape[0], o.shape[1], -1) * g.astype(jnp.float32)

def chunk_mlp(u, v, w_s, b_s, g_norm):
    B, S, _ = u.shape
    vn = rms_norm(v, g_norm).reshape(B, S // BLOCK, BLOCK, N_MLP_GROUPS, MLP_GC)
    f = jnp.einsum('gij,bnjgc->bnigc', w_s, vn) + b_s.T[None, None, :, :, None]
    return u * f.reshape(B, S, MLP_W).astype(u.dtype)

def route(h, w_router, b_router):
    T = h.shape[0]
    scores = jax.nn.sigmoid(jnp.einsum('td,de->te', h, w_router, preferred_element_type=jnp.float32))
    sel = (scores + b_router.astype(jnp.float32)).reshape(T, N_EXPERT_GROUPS, EXPERTS_PER_GROUP)
    group_score = jnp.sum(lax.top_k(sel, TOP_K)[0], axis=-1)
    g_idx = jnp.argmax(group_score, axis=-1)
    in_group = jnp.take_along_axis(sel, g_idx[:, None, None], axis=1)[:, 0]
    _, loc = lax.top_k(in_group, TOP_K)
    eid = g_idx[:, None] * EXPERTS_PER_GROUP + loc
    w = jnp.take_along_axis(scores, eid, axis=-1)
    return eid, w / jnp.sum(w, axis=-1, keepdims=True)

def moe_ffn(h, eid, w, w_gate, w_up, w_down):
    T, D = h.shape
    A = T * TOP_K
    e_flat = eid.reshape(A)
    tok = jnp.arange(A, dtype=jnp.int32) // TOP_K
    order = jnp.argsort(e_flat)
    e_sorted = e_flat[order]
    counts = jnp.bincount(e_flat, length=N_EXPERTS)
    padded = (counts + MOE_BLOCK - 1) // MOE_BLOCK * MOE_BLOCK
    start = jnp.cumsum(counts) - counts
    pend = jnp.cumsum(padded)
    pstart = pend - padded
    dest = pstart[e_sorted] + jnp.arange(A) - start[e_sorted]
    n_blocks = -(-A // MOE_BLOCK) + N_EXPERTS
    P = n_blocks * MOE_BLOCK
    buf_tok = jnp.zeros((P,), jnp.int32).at[dest].set(tok[order])
    xb = h[buf_tok].reshape(n_blocks, MOE_BLOCK, D)
    block_e = jnp.minimum(jnp.searchsorted(pend, jnp.arange(n_blocks) * MOE_BLOCK, side='right'), N_EXPERTS - 1)

    def expert_block(args):
        xi, e = args
        a = jnp.einsum('cd,df->cf', xi, w_gate[e])
        b = jnp.einsum('cd,df->cf', xi, w_up[e])
        return jnp.einsum('cf,fd->cd', jax.nn.silu(a) * b, w_down[e])

    yb = lax.map(expert_block, (xb, block_e)).reshape(P, D)
    contrib = yb[dest] * w.reshape(A)[order][:, None].astype(yb.dtype)
    return jnp.zeros((T, D), h.dtype).at[tok[order]].add(contrib.astype(h.dtype))

def trunk_layer(x, mods, rope_a, rope_r, ctx, lw):
    B, S, _ = x.shape
    shift1, scale1, gate1, shift2, scale2, gate2 = mods
    h = rms_norm(x, lw['norm1']) * (1 + scale1) + shift1
    z = jnp.einsum('bsd,de->bse', h, lw['w_in'])
    sizes = (ATT_Q, ATT_KV, ATT_KV, RET_W, RET_W, RET_W, RET_W, MLP_W, MLP_W, D_MODEL, D_MODEL, D_MODEL)
    cuts = np.cumsum(sizes)[:-1].tolist()
    qa, ka, va, qr, kr, vr, gr, mu, mv, g_att, g_ret, g_mlp = jnp.split(z, cuts, axis=-1)

    qa = rms_norm(qa.reshape(B, S, N_Q_HEADS, HEAD_DIM), lw['q_norm'])
    ka = rms_norm(ka.reshape(B, S, N_KV_HEADS, HEAD_DIM), lw['k_norm'])
    va = va.reshape(B, S, N_KV_HEADS, HEAD_DIM)
    if rope_a is not None:
        qa = apply_rope(qa, *rope_a)
        ka = apply_rope(ka, *rope_a)
    if ctx is None:
        k_all, v_all = ka, va
        s0_f = jnp.zeros((B, N_RET_HEADS, RET_DK, RET_DV), jnp.float32)
        s0_b = s0_f
    else:
        k_ctx, v_ctx, s0_f, s0_b = ctx
        k_all = jnp.concatenate([ka, k_ctx.astype(ka.dtype)], axis=1)
        v_all = jnp.concatenate([va, v_ctx.astype(va.dtype)], axis=1)
    att = block_attention(qa, k_all, v_all)

    qr = qr.reshape(B, S, N_RET_HEADS, RET_DK)
    kr = kr.reshape(B, S, N_RET_HEADS, RET_DK) * (RET_DK ** -0.5)
    vr = vr.reshape(B, S, N_RET_HEADS, RET_DV)
    if rope_r is not None:
        qr = apply_rope(qr, *rope_r)
        kr = apply_rope(kr, *rope_r)
    lg_f = -jnp.exp(lw['ret_decay_fwd'].astype(jnp.float32))
    lg_b = -jnp.exp(lw['ret_decay_bwd'].astype(jnp.float32))
    o, s_f, s_b = bidir_retention(qr, kr, vr, lg_f, lg_b, s0_f, s0_b)
    ret = (head_group_norm(o, lw['ret_gn']) * jax.nn.silu(gr.astype(jnp.float32))).astype(x.dtype)

    cm = chunk_mlp(jax.nn.gelu(mu), jax.nn.gelu(mv), lw['w_spatial'], lw['b_spatial'], lw['mlp_norm'])

    mix = (jax.nn.sigmoid(g_att) * jnp.einsum('bsc,cd->bsd', att, lw['w_att_o'])
           + jax.nn.sigmoid(g_ret) * jnp.einsum('bsc,cd->bsd', ret, lw['w_ret_o'])
           + jax.nn.sigmoid(g_mlp) * jnp.einsum('bsc,cd->bsd', cm, lw['w_mlp_o']))
    x = x + gate1 * jnp.einsum('bsd,de->bse', mix, lw['w_out'])

    h2 = (rms_norm(x, lw['norm2']) * (1 + scale2) + shift2).reshape(B * S, D_MODEL)
    eid, wt = route(h2, lw['w_router'], lw['b_router'])
    y = moe_ffn(h2, eid, wt, lw['w_gate'], lw['w_up'], lw['w_down']).reshape(B, S, D_MODEL)
    x = x + gate2 * y
    return x, ka, va, s_f.astype(x.dtype), s_b.astype(x.dtype)

def setup_inputs(seed: int = 0) -> dict:
    key = jax.random.key(seed)
    ks = jax.random.split(key, 32)
    f32 = jnp.float32

    def nrm(k, shape, scale):
        return jax.random.normal(k, shape, f32) * scale

    decay_base = jnp.log(-jnp.log1p(-(2.0 ** (-5.0 - jnp.arange(N_RET_HEADS, dtype=f32)))))
    return {
        'x_prompt': nrm(ks[0], (BATCH, SEQ, D_MODEL), 1.0),
        'x_sample': nrm(ks[1], (DEC_BATCH, DEC_SEQ, D_MODEL), 1.0),
        'cache_k': nrm(ks[2], (DEC_BATCH, DEPTH, PAST_LEN, N_KV_HEADS, HEAD_DIM), 1.0),
        'cache_v': nrm(ks[3], (DEC_BATCH, DEPTH, PAST_LEN, N_KV_HEADS, HEAD_DIM), 1.0),
        'state_ret_fwd': nrm(ks[4], (DEC_BATCH, DEPTH, N_RET_HEADS, RET_DK, RET_DV), 0.5),
        'state_ret_bwd': nrm(ks[5], (DEC_BATCH, DEPTH, N_RET_HEADS, RET_DK, RET_DV), 0.5),
        'c': nrm(ks[6], (DEC_BATCH, D_MODEL), 1.0),
        'c_ctx': nrm(ks[7], (D_MODEL,), 1.0),
        'w_mod': nrm(ks[8], (DEPTH, D_MODEL, N_MOD * D_MODEL), 0.5 * D_MODEL ** -0.5),
        'b_mod': nrm(ks[9], (DEPTH, N_MOD * D_MODEL), 0.02),
        'norm1': 1.0 + nrm(ks[10], (DEPTH, D_MODEL), 0.02),
        'norm2': 1.0 + nrm(ks[11], (DEPTH, D_MODEL), 0.02),
        'w_in': nrm(ks[12], (DEPTH, D_MODEL, IN_COLS), D_MODEL ** -0.5),
        'q_norm': 1.0 + nrm(ks[13], (DEPTH, HEAD_DIM), 0.02),
        'k_norm': 1.0 + nrm(ks[14], (DEPTH, HEAD_DIM), 0.02),
        'ret_decay_fwd': decay_base[None, :] + nrm(ks[15], (DEPTH, N_RET_HEADS), 0.01),
        'ret_decay_bwd': decay_base[None, :] + nrm(ks[16], (DEPTH, N_RET_HEADS), 0.01),
        'ret_gn': 1.0 + nrm(ks[17], (DEPTH, RET_W), 0.02),
        'mlp_norm': 1.0 + nrm(ks[18], (DEPTH, MLP_W), 0.02),
        'w_spatial': nrm(ks[19], (DEPTH, N_MLP_GROUPS, BLOCK, BLOCK), BLOCK ** -0.5),
        'b_spatial': 1.0 + nrm(ks[20], (DEPTH, N_MLP_GROUPS, BLOCK), 0.02),
        'w_att_o': nrm(ks[21], (DEPTH, ATT_Q, D_MODEL), ATT_Q ** -0.5),
        'w_ret_o': nrm(ks[22], (DEPTH, RET_W, D_MODEL), RET_W ** -0.5),
        'w_mlp_o': nrm(ks[23], (DEPTH, MLP_W, D_MODEL), MLP_W ** -0.5),
        'w_out': nrm(ks[24], (DEPTH, D_MODEL, D_MODEL), D_MODEL ** -0.5),
        'w_router': nrm(ks[25], (D_MODEL, N_EXPERTS), D_MODEL ** -0.5),
        'b_router': nrm(ks[26], (N_EXPERTS,), 0.01),
        'w_gate': nrm(ks[27], (DEPTH, N_EXPERTS, D_MODEL, EXPERT_FF), D_MODEL ** -0.5),
        'w_up': nrm(ks[28], (DEPTH, N_EXPERTS, D_MODEL, EXPERT_FF), D_MODEL ** -0.5),
        'w_down': nrm(ks[29], (DEPTH, N_EXPERTS, EXPERT_FF, D_MODEL), EXPERT_FF ** -0.5),
    }

def reference(x_prompt, x_sample, cache_k, cache_v, state_ret_fwd, state_ret_bwd, c, c_ctx,
              w_mod, b_mod, norm1, norm2, w_in, q_norm, k_norm, ret_decay_fwd, ret_decay_bwd,
              ret_gn, mlp_norm, w_spatial, b_spatial, w_att_o, w_ret_o, w_mlp_o, w_out,
              w_router, b_router, w_gate, w_up, w_down):
    lws = [dict(norm1=norm1[l], norm2=norm2[l], w_in=w_in[l], q_norm=q_norm[l], k_norm=k_norm[l],
                ret_decay_fwd=ret_decay_fwd[l], ret_decay_bwd=ret_decay_bwd[l], ret_gn=ret_gn[l],
                mlp_norm=mlp_norm[l], w_spatial=w_spatial[l], b_spatial=b_spatial[l],
                w_att_o=w_att_o[l], w_ret_o=w_ret_o[l], w_mlp_o=w_mlp_o[l], w_out=w_out[l],
                w_router=w_router, b_router=b_router,
                w_gate=w_gate[l], w_up=w_up[l], w_down=w_down[l]) for l in range(DEPTH)]

    x = x_prompt
    ks, vs, sfs, sbs = [], [], [], []
    for l in range(DEPTH):
        mods = modulation(c_ctx[None, :], w_mod[l], b_mod[l])
        x, k_l, v_l, sf_l, sb_l = trunk_layer(x, mods, None, None, None, lws[l])
        ks.append(k_l)
        vs.append(v_l)
        sfs.append(sf_l)
        sbs.append(sb_l)
    y_prompt = x
    new_k = jnp.stack(ks, axis=1)
    new_v = jnp.stack(vs, axis=1)
    new_sf = jnp.stack(sfs, axis=1)
    new_sb = jnp.stack(sbs, axis=1)

    rows = x_sample.shape[1] // GRID_W
    rope_a = axial_rope(rows, HEAD_DIM)
    rope_r = axial_rope(rows, RET_DK)
    x = x_sample
    for l in range(DEPTH):
        mods = modulation(c, w_mod[l], b_mod[l])
        ctx = (cache_k[:, l], cache_v[:, l], state_ret_fwd[:, l], state_ret_bwd[:, l])
        x, _, _, _, _ = trunk_layer(x, mods, rope_a, rope_r, ctx, lws[l])
    y_sample = x
    return (y_prompt, y_sample, new_k, new_v, new_sf, new_sb)


_drawn_inputs = setup_inputs


def setup_inputs(seed=0):
    import zlib

    import numpy as np

    out = dict(_drawn_inputs(seed))
    spreads = {}
    factors = {'cache_k': 3.056,
     'cache_v': 3.471,
     'q_norm': 13.386,
     'k_norm': 7.987,
     'ret_gn': 20.941,
     'mlp_norm': 10.665,
     'b_spatial': 11.783,
     'norm2': 3.173}
    for name, (base, spread) in spreads.items():
        noise = np.random.default_rng([zlib.crc32(name.encode()), seed]).standard_normal(out[name].shape)
        drawn = base * np.exp(spread * noise) if base else spread * noise
        out[name] = __import__('jax').numpy.asarray(drawn.astype(out[name].dtype))
    for name, factor in factors.items():
        out[name] = (out[name] * factor).astype(out[name].dtype)
    return out
```

```python
from contextlib import ExitStack

import numpy as np

import concourse.bass as bass
from concourse import mybir

F32 = mybir.dt.float32
U32 = mybir.dt.uint32
ALU = mybir.AluOpType
ACT = mybir.ActivationFunctionType
AX = mybir.AxisListType

P = 128
D = 1024
KD = D // P
LAYERS = 2
NT = 5
NS = 4
PROMPT = NT - 1
T = NT * P
GRID_W = 64
EPS = 1e-6
HQ, HKV, DH = 8, 2, 64
HR = 4
NMOD = 6
IN_COLS = 6912
C_QR, C_MU, C_GATE = 768, 2816, 3840
NE, NG, EPG = 16, 4, 4
FF = 512
NBLK = 26
PAIRS = NE // 2
OVER_PAIRS = (NBLK - NE) // 2
SLOT = 4096
BIG = 1.0e30
DEST, N_OVER, E_OVER = NBLK, NBLK + 2 * NT, NBLK + 2 * NT + 1
OVER = 2 * OVER_PAIRS
BLK_IDX = E_OVER + OVER
STATES = [(0, 0), (0, 1), (0, 2), (1, 3), (1, 2), (1, 1), (0, PROMPT), (1, PROMPT)]


def rope_table(dim):
    rows = NS * P // GRID_W
    r = np.repeat(np.arange(rows, dtype=np.float32), GRID_W)
    c = np.tile(np.arange(GRID_W, dtype=np.float32), rows)
    half = dim // 2
    inv = np.float32(10000.0) ** (-np.arange(0, half, 2, dtype=np.float32) / np.float32(half))
    ar, ac = r[:, None] * inv, c[:, None] * inv
    ang = np.concatenate([ar, ar, ac, ac], axis=-1).astype(np.float64)
    sign = np.tile(np.repeat([-1.0, 1.0], dim // 4), 2)
    both = np.stack([np.cos(ang), np.sin(ang) * sign], axis=1).astype(np.float32)
    return both.reshape(NS, P, 2 * dim).transpose(1, 0, 2).reshape(P, -1)


def shape_tables():
    i = np.arange(P, dtype=np.float32)
    row = np.broadcast_to(i, (P, P))
    col = row.T
    persistent = [np.eye(P), (col < row), np.ones((P, P)), rope_table(DH), rope_table(P),
                  np.stack([P - 1 - i, i], 1), np.broadcast_to(np.arange(NE), (P, NE)),
                  np.broadcast_to(np.arange(NE) // EPG, (P, NE)),
                  i[:, None] + P * np.arange(NT)[None, :],
                  np.broadcast_to(P * np.arange(1, NT), (P, NT - 1)),
                  np.broadcast_to(np.arange(NBLK), (P, NBLK))]
    distances = [np.maximum(row - col, 0), (row >= col), np.maximum(col - row, 0), (col >= row),
                 row + 1, P - row]
    return (np.concatenate(persistent, 1).astype(np.float32),
            np.concatenate(distances, 1).astype(np.float32))


PERSISTENT, DISTANCES = shape_tables()


class Signal:

    def __init__(self, sem, per, before=0):
        self.sem, self.per, self.before = sem, per, before

    def at(self, l, n):
        return l * self.per + (self.before + n)


class Steps:

    def __init__(self, eng, done, l, alone):
        self.eng, self.done, self.l, self.n, self.alone = eng, done, l, 0, alone

    def mark(self, ins):
        ins.then_inc(self.done.sem, 1)
        self.n += 1

    def settle(self):
        self.eng.wait_ge(self.done.sem, self.done.at(self.l, self.n))
        self.eng.sem_inc(self.alone, 1)

    def do(self, ins):
        self.mark(ins)
        self.settle()

    def top_up(self):
        assert self.n <= self.done.per
        if self.n < self.done.per:
            self.eng.sem_inc(self.done.sem, self.done.per - self.n)


def trunk(nc, I, O):
    with ExitStack() as ctx:
        def sem(name):
            return ctx.enter_context(nc.semaphore(name))

        def signal(name, per, before=0):
            return Signal(sem(name), per, before)

        def sb(name, cols, dt=F32):
            return ctx.enter_context(nc.sbuf_tensor(name, [P, cols], dt))

        mod_dram = nc.dram_tensor("mod_dram", (LAYERS, 2, NMOD, D), F32, kind="Internal").ap()
        x_dram = nc.dram_tensor("x_dram", (T, D), F32, kind="Internal").ap()
        h2_dram = nc.dram_tensor("h2_dram", (T, D), F32, kind="Internal").ap()
        tok_dram = nc.dram_tensor("tok_dram", (NBLK * P, 1), F32, kind="Internal").ap()
        y_dram = nc.dram_tensor("y_dram", (NBLK * P, D), F32, kind="Internal").ap()

        ring_lo = sb("ring_lo", 4 * SLOT)
        work = sb("work", 17664)
        hT = sb("hT", KD * T)
        branch = sb("branch", 3 * 4 * T)
        const = sb("const", PERSISTENT.shape[1])
        small = sb("small", 3900)
        slots_u = sb("slots_u", BLK_IDX + 2, U32)
        ps = ctx.enter_context(nc.psum_tensor("ps", [P, 8, 512], F32))

        def w_(a, n):
            return work[:, a:a + n]

        slot = [ring_lo[:, s * SLOT:(s + 1) * SLOT] for s in range(4)] + [w_(0, SLOT), w_(SLOT, SLOT)]

        at = [0]

        def take(tensor, n):
            at[0] += n
            return tensor[:, at[0] - n:at[0]]

        ident = take(const, P)
        before = take(const, P)
        ones = take(const, P)
        rope_a = take(const, NS * 2 * DH).rearrange("p (t s d) -> p t s d", t=NS, s=2)
        rope_r = take(const, NS * 2 * P).rearrange("p (t s d) -> p t s d", t=NS, s=2)
        kpos = take(const, 2)
        iota_e = take(const, NE)
        group_e = take(const, NE)
        token_id = take(const, NT)
        full_blocks = take(const, NT - 1)
        iota_b = take(const, NBLK)
        assert at[0] == PERSISTENT.shape[1]
        at[0] = 0
        dec_q = take(small, 2 * HR * P).rearrange("p (f h i) -> p f h i", f=2, h=HR)
        dec_in = take(small, HR * P).rearrange("p (h i) -> p h i", h=HR)
        dec_k = take(small, 2 * HR)
        dec_chunk = take(small, 2 * HR)
        lg = take(small, 2 * HR)
        qk_gain = take(small, 2 * DH)
        ret_gain = take(small, 512)
        mlp_gain = take(small, 512)
        wsT = take(small, 4 * P)
        bs = take(small, 4)
        modc = take(small, 32)
        w_rt = take(small, KD * NE)
        b_rt = take(small, NE)
        st = take(small, 60)
        st2 = take(small, 60)
        bn = take(small, HR * 6)
        bna = take(small, HR * 2)
        negmax = take(small, 40)
        psums = take(small, 40)
        recip = take(small, 40)
        scT = take(small, 16)
        mean_var = take(small, 2 * HR)
        v_cache = take(small, P)
        assert at[0] <= 3900, at[0]

        xr = w_(0, NT * D).rearrange("p (t d) -> p t d", t=NT)
        attT = branch[:, 0:4 * T].rearrange("p (c t) -> p c t", c=4)
        retT = branch[:, 4 * T:8 * T].rearrange("p (c t) -> p c t", c=4)
        cmT = branch[:, 8 * T:12 * T].rearrange("p (c t) -> p c t", c=4)
        aux = branch[:, 8 * T:12 * T]
        dist = aux[:, 0:6 * P]
        ws_raw = aux[:, 768:1280]
        mod_rows = aux[0:32, 1280:1408]
        kc_raw = aux[:, 1408:1536]
        s_raw = aux[:, 1536:2560]
        h3 = hT[:, :].rearrange("p (k t) -> p k t", k=KD)

        const_in = sem("const_in")
        xin = sem("xin")
        cond_t = sem("cond_t")
        cond_s = sem("cond_s")
        mod_mm = sem("mod_mm")
        mod_ev = sem("mod_ev")
        mod_st = sem("mod_st")
        mod_fold = sem("mod_fold")
        tok_zero = sem("tok_zero")
        zeroed = sem("zeroed")
        waited = sem("waited")

        tiles = [("q", 0), ("kv", 1), ("qr", 2), ("kr", 3), ("vr", 0), ("gr", 1), ("mu", 2), ("mv", 3),
                 ("o0", 0), ("g00", 1), ("g01", 2), ("o1", 3), ("g10", 0), ("g11", 1),
                 ("o2", 2), ("g20", 3), ("g21", 0), ("out0", 1), ("out1", 2)]
        slot_of = dict(tiles)
        use_of, uses = {}, [0] * 6
        for name, s in tiles:
            use_of[name] = uses[s]
            uses[s] += 1
        base_use = list(uses)
        per_layer = [u + PAIRS + OVER_PAIRS for u in base_use]
        MODT = 2 * NMOD
        before_use = [MODT * LAYERS // 4] * 4 + [0, 0]
        full = [signal(f"slot{s}_full", 16 * per_layer[s], 16 * before_use[s]) for s in range(6)]

        x_new = signal("x_new", 1)
        aux_in = signal("aux_in", 16 * 15)
        xs_out = signal("xs_out", 16)
        v_step = signal("dve_step", 460)
        a_step = signal("act_step", 80)
        g_step = signal("pool_step", 64)
        ssq1 = signal("ssq1", 1)
        rt_a = signal("roots", 9)
        ms_v = signal("mean_squares", 9)
        xn_v = signal("xn_ready", NT)
        tr_p = signal("xn_turned", KD)
        h_a = signal("h_sample", KD)
        h_v = signal("h_prompt", KD)
        au_p = signal("aux_turned", 2)
        mc_v = signal("mod_cols", 1)
        ws_v = signal("ws_ready", 1)
        dec_a = signal("decays_exp", 1)
        dec_v = signal("decays_ready", 1)
        z_p = signal("z_product", 25)
        z_a = signal("z_taken", 25)
        qk_v = signal("qk_ready", NT)
        kv_out = signal("kv_out", 32)
        rr_v = signal("ret_roped", NS)
        qt_p = signal("qk_turned", 6)
        qt_a = signal("qkT_ready", 6)
        s_p = signal("scores", 40)
        mx_v = signal("max_ready", 40)
        e_a = signal("probs", 40)
        pt_p = signal("probs_turned", 40)
        pt_a = signal("probsT_ready", 40)
        pv_p = signal("pv_done", 40)
        at_v = signal("att_ready", NT)
        at_p = signal("att_turned", NT)
        at_a = signal("attT_ready", NT)
        kd_g = signal("kdec_ready", 8)
        kv_p = signal("kv_product", 8)
        kv_v = signal("state_ready", 8)
        st_a = signal("start_states", 2)
        st_out = signal("state_out", 32)
        rq_p = signal("ret_q_turned", NT)
        rk_p = signal("ret_k_turned", NT)
        rq_v = signal("ret_qT", NT)
        rk_a = signal("ret_kT", NT)
        in_p = signal("inner_product", NT)
        in_v = signal("inner_ready", NT)
        gr_p = signal("gr_product", NT)
        gr_a = signal("gr_silu", NT)
        o_p = signal("ret_out", NT)
        rn_v = signal("ret_normed", NT)
        rt_p = signal("ret_turned", NT)
        rt_ev = signal("retT_ready", NT)
        m_p = signal("mlp_product", 10)
        m_a = signal("mlp_gelu", 10)
        vn_v = signal("mlp_normed", NT)
        f_p = signal("spatial", NT)
        cm_v = signal("cm_ready", NT)
        cm_p = signal("cm_turned", NT)
        cm_a = signal("cmT_ready", NT)
        g_p = signal("gate_product", 24)
        g_a = signal("gate_sigmoid", 24)
        o3_p = signal("branch_product", 24)
        mix_v = signal("mix_ready", 24)
        res_in = signal("residual_in", 48)
        w_p = signal("out_product", 10)
        x_v = signal("x_mid", 10)
        xm_out = signal("x_mid_out", 16)
        mod2_in = signal("mod2_in", 64)
        ssq2 = signal("ssq2", 1)
        h2_v = signal("h2_ready", NT)
        h2_out = signal("h2_out", 16)
        h2_p = signal("h2_turned", KD)
        h2_a = signal("h2T_sample", KD)
        h2_q = signal("h2T_prompt", KD)
        lo_p = signal("logits", 1)
        sc_a = signal("scores_ready", 1)
        oh_v = signal("one_hots", 1)
        rk_p2 = signal("ranks", 1)
        de_v = signal("dest_ready", 1)
        tok_out = signal("tok_out", 16 * 2 * NT)
        tok_in = signal("tok_in", 16)
        tk_p = signal("tok_turned", 1)
        tk_v = signal("tok_ready", 1)
        NB2 = 2 * (PAIRS + OVER_PAIRS)
        idx_g = signal("block_idx", NB2)
        xb_in = [signal(f"xb_in{b}", 16 * NB2 // 2) for b in range(2)]
        xt_p = signal("xb_turned", NB2, 2)
        xt_a = signal("xbT_ready", NB2)
        a_p = signal("gate_up", 2 * NB2)
        si_a = signal("silu_gate", NB2)
        hd_v = signal("hidden", NB2)
        ht_p = signal("hidden_turned", NB2)
        ht_v = signal("hiddenT", NB2)
        y_p = signal("down", 2 * NB2)
        y_a = signal("y_ready", 2 * NB2, 1)
        y_out = [signal(f"y_out{b}", 16 * NB2 // 2, 16) for b in range(2)]
        cx_in = signal("combine_x_in", 16)
        g2_in = signal("gate2_in", 32)
        y1_in = [signal(f"y1_in{b}", 16 * (3 if b == 0 else 2)) for b in range(2)]
        y2_in = [signal(f"y2_in{b}", 16 * (3 if b == 0 else 2)) for b in range(2)]
        cb_v = signal("combined", NT)
        fin_out = sem("fin_out")

        def w_alone(eng, sig, l, n):
            eng.wait_ge(sig.sem, sig.at(l, n))
            eng.sem_inc(waited, 1)

        def w(eng, sig, l, n):
            if eng is nc.gpsimd or eng is nc.sync:
                w_alone(eng, sig, l, n)
            else:
                eng.wait_ge(sig.sem, sig.at(l, n))

        def last_users():
            z = {"q": (z_p, NT), "kv": (z_p, 2 * NT), "qr": (z_p, 3 * NT), "kr": (z_p, 4 * NT),
                 "vr": (z_p, 5 * NT), "gr": (gr_p, NT), "mu": (m_p, NT), "mv": (m_p, 2 * NT),
                 "out0": (w_p, NT), "out1": (w_p, 2 * NT)}
            for b in range(3):
                z[f"g{b}0"] = (g_p, 8 * b + 4)
                z[f"g{b}1"] = (g_p, 8 * b + 8)
                z[f"o{b}"] = (o3_p, 8 * b + 8)
            return z

        users = last_users()
        at_slot = [[n for n, s in tiles if s == q] for q in range(6)]

        block = ctx.enter_context(nc.Block())

        @block.sync
        def _(sp):
            def load(s, src, nk, cols):
                return sp.dma_start(slot[s][:, 0:nk * cols].rearrange("p (k c) -> p k c", k=nk), src)

            def rows(ap):
                return ap.rearrange("(k p) c -> p k c", p=P)

            for n in range(LAYERS * MODT):
                if n >= 4:
                    sp.wait_ge(mod_mm, n - 3)
                l, t = divmod(n, MODT)
                load(n % 4, rows(I["w_mod"][l, :, t * 512:(t + 1) * 512]), KD, 512).then_inc(full[n % 4].sem, 16)

            sp.wait_ge(mod_mm, LAYERS * MODT)
            with sp.Fori(0, LAYERS) as l:
                def dyn(ap):
                    return ap[bass.ds(l, 1)]

                def win(c0, cols):
                    return dyn(I["w_in"])[:, :, c0:c0 + cols].rearrange("o (k p) c -> p (o k) c", p=P)

                for name, s in tiles:
                    if use_of[name] > 0:
                        prev = at_slot[s][use_of[name] - 1]
                        w(sp, users[prev][0], l, users[prev][1])
                    cols, nk = 512, KD
                    if name == "q":
                        src = win(0, 512)
                    elif name == "kv":
                        src, cols = win(512, 256), 256
                    elif name in ("qr", "kr", "vr", "gr"):
                        src = win(C_QR + 512 * ("qr", "kr", "vr", "gr").index(name), 512)
                    elif name in ("mu", "mv"):
                        src = win(C_MU + 512 * ("mu", "mv").index(name), 512)
                    elif name[0] == "g":
                        src = win(C_GATE + D * int(name[1]) + 512 * int(name[2]), 512)
                    elif name[:3] == "out":
                        h = int(name[3])
                        src = dyn(I["w_out"])[:, :, 512 * h:512 * h + 512].rearrange("o (k p) c -> p (o k) c", p=P)
                    else:
                        wo = I[("w_att_o", "w_ret_o", "w_mlp_o")[int(name[1])]]
                        src, nk, cols = dyn(wo).rearrange("o (k p) c -> p (o k) c", p=P), 4, D
                    load(s, src, nk, cols).then_inc(full[s].sem, 16)

                def expert(e, half):
                    for i, (nm, nk, cols) in enumerate((("w_gate", KD, FF), ("w_up", KD, FF), ("w_down", 4, D))):
                        src = dyn(I[nm])[:, bass.ds(e, 1)].rearrange("o e (k p) c -> p (o e k) c", p=P)
                        yield 3 * half + i, src, nk, cols

                done = {0: users["g21"], 1: users["out0"], 2: users["out1"], 3: users["g20"]}
                for half in range(2):
                    for s, src, nk, cols in expert(half, half):
                        if s < 4:
                            w(sp, done[s][0], l, done[s][1])
                        elif s == 4:
                            w(sp, h2_v, l, NT)
                            w(sp, xm_out, l, 16)
                        load(s, src, nk, cols).then_inc(full[s].sem, 16)
                with sp.Fori(1, PAIRS) as j:
                    for half in range(2):
                        for s, src, nk, cols in expert(2 * j + half, half):
                            if s % 3 < 2:
                                sp.wait_ge(a_p.sem, a_p.at(l, 0) + 4 * j + (2 * half + s % 3 - 3))
                                sp.sem_inc(waited, 1)
                            else:
                                sp.wait_ge(y_p.sem, y_p.at(l, 0) + 4 * j + (2 * half - 2))
                                sp.sem_inc(waited, 1)
                            load(s, src, nk, cols).then_inc(full[s].sem, 16)
                w(sp, tk_v, l, 1)
                w(sp, y_p, l, 4 * PAIRS)
                n_over = sp.value_load(slots_u[0:1, N_OVER:N_OVER + 1], min_val=0, max_val=9)
                with sp.If(n_over > 0):
                    with sp.Fori(0, OVER_PAIRS) as j:
                        for half in range(2):
                            col = E_OVER + 2 * j + half
                            e = sp.value_load(slots_u[0:1, bass.ds(col, 1)], min_val=0, max_val=NE - 1)
                            for s, src, nk, cols in expert(e, half):
                                if s % 3 < 2:
                                    sp.wait_ge(a_p.sem, a_p.at(l, 4 * PAIRS) + 4 * j + (2 * half + s % 3 - 3))
                                    sp.sem_inc(waited, 1)
                                else:
                                    sp.wait_ge(y_p.sem, y_p.at(l, 4 * PAIRS) + 4 * j + (2 * half - 2))
                                    sp.sem_inc(waited, 1)
                                load(s, src, nk, cols).then_inc(full[s].sem, 16)
                with sp.Else():
                    for s in range(6):
                        sp.sem_inc(full[s].sem, 16 * OVER_PAIRS)
                w(sp, y_p, l, 2 * NB2)

        xn = w_(6144, NT * D).rearrange("p (t d) -> p t d", t=NT)
        sq1 = w_(5120, D)
        zr = w_(0, NT * 3 * 512).rearrange("p (t i c) -> p t i c", t=NT, i=3)
        qT = w_(7680, 4 * T).rearrange("p (i t) -> p i t", i=4)
        kT = w_(10240, 768)
        zq = w_(11264, NT * 768).rearrange("p (t c) -> p t c", t=NT)
        prob = [w_(15104 + 640 * b, 640) for b in range(2)]
        dec_tmp = w_(15104, 1024).rearrange("p (f h i) -> p f h i", f=2, h=HR)
        rope_tmp = w_(15104, 1024)
        probT = [w_(16384 + 640 * b, 640) for b in range(2)]
        qk_tmp = w_(16384, 640)
        st_tmp = w_(7680, 512)
        st_buf = [w_(7680, 512), w_(8192, 512)]
        kdec = [w_(8704, 512), w_(9216, 512)]
        o_tmp = w_(8704, 512)
        sb_st = [w_(9728 + 512 * n, 512) for n in range(NS)]
        sf_st = [w_(11776 + 512 * n, 512) for n in range(NS)]
        rqT, rqTf, rqTb, rkT = (w_(13824 + 512 * n, 512).rearrange("p (h i) -> p h i", h=HR) for n in range(4))
        inner = [w_(15872 + 512 * b, 512).rearrange("p (h i) -> p h i", h=HR) for b in range(2)]
        sgr = w_(16896, 512)
        gu = w_(0, NT * 512).rearrange("p (t c) -> p t c", t=NT)
        gv = w_(2560, NT * 512).rearrange("p (t c) -> p t c", t=NT)
        cmb = [w_(5120 + 512 * b, 512) for b in range(2)]
        mlp_tmp = w_(8704, 512)
        mixT = w_(8192, KD * T).rearrange("p (k t) -> p k t", k=KD)
        sg = [w_(13312 + 640 * b, 640) for b in range(2)]
        mix_tmp = w_(14592, 640)
        gate1 = w_(15232, 2 * D).rearrange("p (s d) -> p s d", s=2)
        out_tmp = [hT[:, 512 * b:512 * b + 512] for b in range(2)]
        sq2 = hT[:, 0:D]
        h2 = w_(8192, NT * D).rearrange("p (t d) -> p t d", t=NT)
        gain2 = w_(13312, 2 * D).rearrange("p (s d) -> p s d", s=2)
        shift2 = w_(15360, 2 * D).rearrange("p (s d) -> p s d", s=2)
        xb = [w_(8192 + D * b, D) for b in range(2)]
        xbT = [w_(10240 + D * b, D) for b in range(2)]
        sa = [w_(12288 + 512 * b, 512) for b in range(2)]
        hd = [w_(13312 + 512 * b, 512) for b in range(2)]
        hdT = [w_(14336 + 512 * b, 512) for b in range(2)]
        yb = [w_(15360 + D * b, D) for b in range(2)]
        y1 = [w_(8192 + 2 * D * b, D) for b in range(2)]
        y2 = [w_(8192 + 2 * D * b + D, D) for b in range(2)]
        gate2 = w_(12288, 2 * D).rearrange("p (s d) -> p s d", s=2)
        cb_tmp = w_(14336, D)
        mod_row = w_(5120, NMOD * D)
        b_mod = [w_(11264, NMOD * D), branch[:, 0:NMOD * D]]
        norm_row = hT[:, 0:4 * D].rearrange("p (l n d) -> p l n d", l=LAYERS, n=2)
        zeros = hT[:, 4 * D + P:4 * D + P + 512]
        cond_rows = hT[0:16, 4 * D:4 * D + P]
        at[0] = 0
        (r_sc, r_sel, r_mask, r_oh0, r_oh1, r_oh, r_tmp, r_masked) = (
            take(branch, NT * NE).rearrange("p (t e) -> p t e", t=NT) for _ in range(8))
        r_m1, r_n1, r_m2, r_n2 = (take(branch, NT * NG) for _ in range(4))
        r_gs = take(branch, NT * 8).rearrange("p (t e) -> p t e", t=NT)
        r_top = take(branch, NT * 8).rearrange("p (t e) -> p t e", t=NT)
        r_gi = take(branch, NT * 8).bitcast(U32).rearrange("p (t e) -> p t e", t=NT)
        r_ei = take(branch, NT * 8).bitcast(U32).rearrange("p (t e) -> p t e", t=NT)
        r_gf = take(branch, NT)
        r_ef = [take(branch, NT) for _ in range(2)]
        r_w = [take(branch, NT) for _ in range(2)]
        r_wn = [take(branch, NT) for _ in range(2)]
        r_rank = [take(branch, NT) for _ in range(2)]
        r_dest = [take(branch, NT) for _ in range(2)]
        r_hi, r_ob, r_sum = (take(branch, NT) for _ in range(3))
        r_cnt, r_ov, r_c0, r_c1, r_ex = (take(branch, NE) for _ in range(5))
        r_le = take(branch, OVER * NE).rearrange("p (b e) -> p b e", b=OVER)
        r_eo = take(branch, OVER)
        r_tok = take(branch, P)
        assert at[0] <= 8 * T

        def flat(a):
            return a.rearrange("p a b -> p (a b)")

        def heads(a):
            return a.rearrange("p (h i) -> p h i", h=HR)

        def bank(b, n=512):
            return ps[:, b, 0:n]

        def two(b):
            return ps[:, b:b + 2, :].rearrange("p b c -> p (b c)")[:, 0:T]

        def cond_of(tt):
            return 1 if tt == PROMPT else 0

        def tok(tt):
            return slice(tt * P, (tt + 1) * P)

        @block.tensor
        def _(pe):
            def mm(out, lhsT, rhs, k, n):
                return pe.matmul(out, lhsT, rhs, start=(k == 0), stop=(k == n - 1))

            pe.wait_ge(const_in, 16 * 9)
            pe.transpose(ps[:, 7, 0:16], cond_rows, ident[0:16, 0:16]).then_inc(cond_t, 1)
            pe.wait_ge(cond_s, 1)
            for n in range(LAYERS * MODT):
                pe.wait_ge(full[n % 4].sem, 16 * (n // 4 + 1))
                if n >= 4:
                    pe.wait_ge(mod_ev, n - 3)
                for k in range(KD):
                    i = mm(ps[0:2, n % 4, :], scT[:, k:16:KD], slot[n % 4][:, k * 512:(k + 1) * 512], k, KD)
                i.then_inc(mod_mm, 1)
            pe.wait_ge(mod_ev, LAYERS * MODT)

            with pe.Fori(0, LAYERS) as l:
                def loaded(name):
                    s = slot_of[name]
                    w(pe, full[s], l, 16 * (use_of[name] + 1))
                    return slot[s]

                w_alone(pe, aux_in, l, aux_in.per)
                pe.transpose(ps[:, 4, 0:32], mod_rows, ident[0:32, 0:32]).then_inc(au_p.sem, 1)
                for g in range(4):
                    i = pe.transpose(ps[:, 5, g * P:(g + 1) * P], ws_raw[:, g * P:(g + 1) * P], ident)
                i.then_inc(au_p.sem, 1)
                w(pe, xn_v, l, NT)
                for k in range(KD):
                    if k >= 2:
                        w(pe, h_a, l, k - 1)
                        w(pe, h_v, l, k - 1)
                    for tt in range(NT):
                        out = ps[:, k % 2, tok(tt)] if tt < NS else ps[:, 2 + k % 2, 0:P]
                        i = pe.transpose(out, xn[:, tt, k * P:(k + 1) * P], ident)
                    i.then_inc(tr_p.sem, 1)
                w(pe, h_a, l, KD)
                w(pe, h_v, l, KD)
                for s, (name, cols) in enumerate((("q", 512), ("kv", 256), ("qr", 512), ("kr", 512), ("vr", 512))):
                    wt = loaded(name)
                    for tt in range(NT):
                        g = s * NT + tt
                        if g >= 4:
                            w(pe, z_a, l, g - 3)
                        for k in range(KD):
                            i = mm(bank(g % 4, cols), h3[:, k, tok(tt)], wt[:, k * cols:(k + 1) * cols], k, KD)
                        i.then_inc(z_p.sem, 1)
                w(pe, mc_v, l, 1)
                w(pe, ws_v, l, 1)
                for tt in range(NT + 1):
                    if tt >= 2:
                        w(pe, qt_a, l, tt - 1)
                    if tt < NT:
                        w(pe, qk_v, l, tt + 1)
                        for i4 in range(4):
                            pe.transpose(ps[:, 4 + tt % 2, i4 * P:(i4 + 1) * P], zq[:, tt, i4 * P:(i4 + 1) * P], ident)
                    src = zq[:, tt, 512:640] if tt < NT else kc_raw
                    pe.transpose(ps[:, 6 + tt % 2, 0:P], src, ident).then_inc(qt_p.sem, 1)

                w(pe, z_a, l, 5 * NT)
                w(pe, qt_a, l, NT + 1)

                def score(u):
                    tt, h = divmod(u, HQ)
                    half, i4 = divmod(h, 4)
                    b = 2 * (u % 2)
                    if u >= 2:
                        w(pe, e_a, l, u - 1)
                    part = slice(half * DH, half * DH + DH)
                    if tt < NS:
                        pe.matmul(bank(b), qT[part, i4, tok(tt)], kT[part, 0:512], start=True, stop=True)
                        i = pe.matmul(bank(b + 1, P), qT[part, i4, tok(tt)], kT[part, 512:640], start=True, stop=True)
                    else:
                        i = pe.matmul(bank(b, P), qT[part, i4, tok(tt)], kT[part, 640:768], start=True, stop=True)
                    i.then_inc(s_p.sem, 1)

                def turn_probs(u):
                    w(pe, e_a, l, u + 1)
                    if u >= 1:
                        w(pe, pt_a, l, u)
                    nk = 5 if u // HQ < NS else 1
                    for c in range(nk):
                        out = ps[:, 4, c * P:(c + 1) * P] if c < 4 else ps[:, 5, 0:P]
                        i = pe.transpose(out, prob[u % 2][:, c * P:(c + 1) * P], ident)
                    i.then_inc(pt_p.sem, 1)

                def values(u):
                    tt, h = divmod(u, HQ)
                    kv = 640 + DH * (h // 4)
                    w(pe, pt_a, l, u + 1)
                    if h == 0 and tt >= 2:
                        w(pe, at_a, l, tt - 1)
                    nk = 5 if tt < NS else 1
                    for c in range(nk):
                        if tt == PROMPT:
                            v = zq[:, PROMPT, kv:kv + DH]
                        elif c < NS:
                            v = zq[:, c, kv:kv + DH]
                        else:
                            v = v_cache[:, kv - 640:kv - 640 + DH]
                        i = mm(ps[:, 6 + tt % 2, h * DH:(h + 1) * DH], probT[u % 2][:, c * P:(c + 1) * P], v, c, nk)
                    i.then_inc(pv_p.sem, 1)

                def turn_att(tt):
                    w(pe, at_v, l, tt + 1)
                    for c in range(4):
                        i = pe.transpose(ps[:, 6 + tt % 2, c * P:(c + 1) * P], zq[:, tt, c * P:(c + 1) * P], ident)
                    i.then_inc(at_p.sem, 1)

                NU = NT * HQ
                score(0)
                for u in range(NU):
                    if u + 1 < NU:
                        score(u + 1)
                    turn_probs(u)
                    if u >= 1:
                        values(u - 1)
                    if u >= 11 and (u - 11) % HQ == 0:
                        turn_att((u - 11) // HQ)
                values(NU - 1)
                turn_att(NT - 1)

                w(pe, e_a, l, NU)
                for n, (_, tt) in enumerate(STATES):
                    w(pe, kd_g, l, n + 1)
                    if n >= 2:
                        w(pe, kv_v, l, n - 1)
                    for h in range(HR):
                        hs = slice(h * P, (h + 1) * P)
                        i = pe.matmul(ps[:, n % 2, hs], kdec[n % 2][:, hs], zr[:, tt, 2, hs], start=True, stop=True)
                    i.then_inc(kv_p.sem, 1)

                def turn_ret(tt):
                    w(pe, rn_v, l, tt + 1)
                    if tt >= 1:
                        w(pe, rt_ev, l, tt)
                    for c in range(4):
                        i = pe.transpose(ps[:, 7, c * P:(c + 1) * P], o_tmp[:, c * P:(c + 1) * P], ident)
                    i.then_inc(rt_p.sem, 1)

                w(pe, pt_a, l, NU)
                w(pe, at_a, l, NT)
                wt = loaded("gr")
                w(pe, kv_v, l, 2 * (NS - 1))
                w(pe, st_a, l, 2)
                for tt in range(NT):
                    for src, b, sig_p, sig_e in ((0, 2, rq_p, rq_v), (1, 3, rk_p, rk_a)):
                        if tt >= 1:
                            w(pe, sig_e, l, tt)
                        for h in range(HR):
                            i = pe.transpose(ps[:, b, h * P:(h + 1) * P], zr[:, tt, src, h * P:(h + 1) * P], ident)
                        i.then_inc(sig_p.sem, 1)
                    if tt >= 1:
                        w(pe, gr_a, l, tt)
                    for k in range(KD):
                        i = mm(bank(5), h3[:, k, tok(tt)], wt[:, k * 512:(k + 1) * 512], k, KD)
                    i.then_inc(gr_p.sem, 1)
                    w(pe, rq_v, l, tt + 1)
                    w(pe, rk_a, l, tt + 1)
                    if tt >= 1:
                        w(pe, in_v, l, tt)
                    for h in range(HR):
                        i = pe.matmul(ps[:, 4, h * P:(h + 1) * P], rkT[:, h, :], rqT[:, h, :], start=True, stop=True)
                    i.then_inc(in_p.sem, 1)
                    if tt >= 1:
                        turn_ret(tt - 1)
                    w(pe, in_v, l, tt + 1)
                    for h in range(HR):
                        hs = slice(h * P, (h + 1) * P)
                        n = 3 if tt < NS else 1
                        i = mm(ps[:, 6, hs], inner[tt % 2][:, h, :], zr[:, tt, 2, hs], 0, n)
                        if tt < NS:
                            mm(ps[:, 6, hs], rqTf[:, h, :], sf_st[tt][:, hs], 1, n)
                            i = mm(ps[:, 6, hs], rqTb[:, h, :], sb_st[tt][:, hs], 2, n)
                    i.then_inc(o_p.sem, 1)
                turn_ret(NT - 1)

                w(pe, kv_v, l, 8)
                w(pe, rq_v, l, NT)
                w(pe, rk_a, l, NT)
                for s, name in enumerate(("mu", "mv")):
                    wt = loaded(name)
                    for tt in range(NT):
                        g = s * NT + tt
                        if g >= 4:
                            w(pe, m_a, l, g - 3)
                        for k in range(KD):
                            i = mm(bank(g % 4), h3[:, k, tok(tt)], wt[:, k * 512:(k + 1) * 512], k, KD)
                        i.then_inc(m_p.sem, 1)
                w(pe, in_v, l, NT)
                w(pe, gr_a, l, NT)
                w(pe, rt_ev, l, NT)

                def turn_cm(tt):
                    w(pe, cm_v, l, tt + 1)
                    if tt >= 2:
                        w(pe, cm_a, l, tt - 1)
                    for c in range(4):
                        i = pe.transpose(ps[:, 6 + tt % 2, c * P:(c + 1) * P], cmb[tt % 2][:, c * P:(c + 1) * P], ident)
                    i.then_inc(cm_p.sem, 1)

                for tt in range(NT):
                    w(pe, vn_v, l, tt + 1)
                    if tt >= 2:
                        w(pe, cm_v, l, tt - 1)
                    for g in range(4):
                        gs = slice(g * P, (g + 1) * P)
                        i = pe.matmul(ps[:, 4 + tt % 2, gs], wsT[:, gs], gv[:, tt, gs], start=True, stop=True)
                    i.then_inc(f_p.sem, 1)
                    if tt >= 1:
                        turn_cm(tt - 1)
                turn_cm(NT - 1)

                w(pe, m_a, l, 2 * NT)
                w(pe, cm_v, l, NT)
                w(pe, cm_a, l, NT)
                for br, src in enumerate((attT, retT, cmT)):
                    wo = None
                    for c in range(KD):
                        n = 8 * br + c
                        if c % 4 == 0:
                            wg = None
                        if c == 0:
                            wo = loaded(f"o{br}")
                        if wg is None:
                            wg = loaded(f"g{br}{c // 4}")
                        b = 2 * (n % 2)
                        if n >= 2:
                            w(pe, g_a, l, n - 1)
                        gc = (c % 4) * P
                        for k in range(KD):
                            mm(bank(b), wg[:, k * 512 + gc:k * 512 + gc + P], h3[:, k, 0:512], k, KD)
                        for k in range(KD):
                            i = mm(bank(b + 1, P), wg[:, k * 512 + gc:k * 512 + gc + P], h3[:, k, 512:640], k, KD)
                        i.then_inc(g_p.sem, 1)
                        if n >= 2:
                            w(pe, mix_v, l, n - 1)
                        for k in range(4):
                            mm(bank(4 + b), wo[:, k * D + c * P:k * D + (c + 1) * P], src[:, k, 0:512], k, 4)
                        for k in range(4):
                            i = mm(bank(5 + b, P), wo[:, k * D + c * P:k * D + (c + 1) * P], src[:, k, 512:640], k, 4)
                        i.then_inc(o3_p.sem, 1)
                w(pe, mix_v, l, 24)
                for half in range(2):
                    wt = loaded(f"out{half}")
                    for tt in range(NT):
                        q = half * NT + tt
                        if q >= 4:
                            w(pe, x_v, l, q - 3)
                        for k in range(KD):
                            i = mm(bank(q % 4), mixT[:, k, tok(tt)], wt[:, k * 512:(k + 1) * 512], k, KD)
                        i.then_inc(w_p.sem, 1)
                w(pe, h2_v, l, NT)
                for k in range(KD):
                    if k >= 2:
                        w(pe, h2_a, l, k - 1)
                        w(pe, h2_q, l, k - 1)
                    for tt in range(NT):
                        out = ps[:, 4 + k % 2, tok(tt)] if tt < NS else ps[:, 6 + k % 2, 0:P]
                        i = pe.transpose(out, h2[:, tt, k * P:(k + 1) * P], ident)
                    i.then_inc(h2_p.sem, 1)
                w(pe, h2_a, l, KD)
                w(pe, h2_q, l, KD)
                for tt in range(NT):
                    for k in range(KD):
                        i = mm(ps[:, 0, tt * NE:(tt + 1) * NE], h3[:, k, tok(tt)], w_rt[:, k * NE:(k + 1) * NE], k, KD)
                i.then_inc(lo_p.sem, 1)
                w(pe, oh_v, l, 1)
                for tt in range(NT):
                    out = ps[:, 1, tt * NE:(tt + 1) * NE]
                    for t2 in range(tt):
                        mm(out, ones, r_oh[:, t2, :], t2, tt + 1)
                    mm(out, before, r_oh[:, tt, :], tt, tt + 1)
                for tt in range(NT):
                    i = mm(ps[:, 1, 80:96], ones, r_oh[:, tt, :], tt, NT)
                i.then_inc(rk_p2.sem, 1)
                w_alone(pe, tok_in, l, 16)
                pe.transpose(ps[:, 2, 0:NBLK], r_tok[0:NBLK, :], ident[0:NBLK, 0:NBLK]).then_inc(tk_p.sem, 1)
                w_alone(pe, tk_v, l, 1)

                def pair(j, n0, u0):
                    def got(s):
                        pe.wait_ge(full[s].sem, full[s].at(l, 16 * (base_use[s] + u0 + 1)) + 16 * j)
                        return slot[s]

                    def turn_x(b):
                        pe.wait_ge(xb_in[b].sem, xb_in[b].at(l, 16 * (n0 // 2 + 1)) + 16 * j)
                        for c in range(KD):
                            i = pe.transpose(ps[:, c // 4, (c % 4) * P:(c % 4 + 1) * P],
                                             xb[b][:, c * P:(c + 1) * P], ident)
                        i.then_inc(xt_p.sem, 1)

                    def up(b, i2):
                        wt = got(3 * b + i2)
                        for k in range(KD):
                            i = mm(bank(2 + 2 * i2 + b), xbT[b][:, k * P:(k + 1) * P], wt[:, k * 512:(k + 1) * 512], k, KD)
                        i.then_inc(a_p.sem, 1)

                    def turn_h(b):
                        pe.wait_ge(hd_v.sem, hd_v.at(l, n0 + b + 1) + 2 * j)
                        pe.wait_ge(y_a.sem, y_a.at(l, 2 * (n0 + b)) + 4 * j)
                        for c in range(4):
                            i = pe.transpose(ps[:, 6, c * P:(c + 1) * P], hd[b][:, c * P:(c + 1) * P], ident)
                        i.then_inc(ht_p.sem, 1)

                    def down(b):
                        pe.wait_ge(ht_v.sem, ht_v.at(l, n0 + b + 1) + 2 * j)
                        wt = got(3 * b + 2)
                        for half in range(2):
                            for k in range(4):
                                i = mm(bank(7 - half), hdT[b][:, k * P:(k + 1) * P],
                                       wt[:, k * D + half * 512:k * D + half * 512 + 512], k, 4)
                            i.then_inc(y_p.sem, 1)

                    turn_x(0)
                    pe.wait_ge(xt_a.sem, xt_a.at(l, n0 + 1) + 2 * j)
                    up(0, 0)
                    up(0, 1)
                    turn_x(1)
                    pe.wait_ge(xt_a.sem, xt_a.at(l, n0 + 2) + 2 * j)
                    up(1, 0)
                    turn_h(0)
                    up(1, 1)
                    down(0)
                    turn_h(1)
                    down(1)

                with pe.Fori(0, PAIRS) as j:
                    pair(j, 0, 0)
                n_over = pe.value_load(slots_u[0:1, N_OVER:N_OVER + 1], min_val=0, max_val=9)
                w_alone(pe, y_p, l, 4 * PAIRS)
                with pe.If(n_over > 0):
                    with pe.Fori(0, OVER_PAIRS) as j:
                        pair(j, NE, PAIRS)
                with pe.Else():
                    pe.sem_inc(xt_p.sem, OVER)
                    pe.sem_inc(a_p.sem, 2 * OVER)
                    pe.sem_inc(ht_p.sem, OVER)
                    pe.sem_inc(y_p.sem, 2 * OVER)
                w_alone(pe, x_new, l, 2)

        @block.scalar
        def _(act):
            A = act.activation
            act.wait_ge(cond_t, 1)
            A(scT, ps[:, 7, 0:16], ACT.Silu).then_inc(cond_s, 1)

            with act.Fori(0, LAYERS) as l:
                step = Steps(act, a_step, l, waited)
                roots = [0]

                def root(ap):
                    roots[0] += 1
                    w(act, ms_v, l, roots[0])
                    A(ap, ap, ACT.Sqrt).then_inc(rt_a.sem, 1)

                w(act, x_new, l, 1)
                for tt in range(NT):
                    i = A(sq1, xr[:, tt, :], ACT.Square, accum_out=st[:, tt:tt + 1])
                    step.do(i) if tt < NT - 1 else i.then_inc(ssq1.sem, 1)
                root(st[:, 0:NT])
                w(act, mc_v, l, 1)
                for k in range(KD):
                    w(act, tr_p, l, k + 1)
                    A(h3[:, k, 0:512], bank(k % 2), ACT.Identity, bias=modc[:, k:k + 1],
                      scale=modc[:, KD + k:KD + k + 1]).then_inc(h_a.sem, 1)
                w(act, aux_in, l, aux_in.per)
                step.do(A(lg, lg, ACT.Exp))
                step.do(A(lg, lg, ACT.Copy, scale=-1.0))
                for f in range(2):
                    for h in range(HR):
                        s_ = lg[:, 4 * f + h:4 * f + h + 1]
                        A(dec_q[:, f, h, :], dist[:, (4 + f) * P:(5 + f) * P], ACT.Exp, scale=s_)
                        A(dec_tmp[:, f, h, :], dist[:, 2 * f * P:(2 * f + 1) * P], ACT.Exp, scale=s_)
                    A(dec_k[:, 4 * f:4 * f + 4], lg[:, 4 * f:4 * f + 4], ACT.Exp, scale=kpos[:, f:f + 1])
                A(dec_chunk, lg, ACT.Exp, scale=float(P)).then_inc(dec_a.sem, 1)
                for g in range(5 * NT):
                    s, tt = divmod(g, NT)
                    w(act, z_p, l, g + 1)
                    if s == 0:
                        dst, n = zq[:, tt, 0:512], 512
                    elif s == 1:
                        dst, n = zq[:, tt, 512:768], 256
                    else:
                        dst, n = zr[:, tt, s - 2, :], 512
                    if g == 2 * NT:
                        w(act, xs_out, l, 16)
                    A(dst, bank(g % 4, n), ACT.Copy, scale=(float(P) ** -0.5 if s == 3 else 1.0)).then_inc(z_a.sem, 1)
                    if g == 2 * NT + 1:
                        root(st[:, 0:50])
                for tt in range(NT + 1):
                    w(act, qt_p, l, tt + 1)
                    if tt < NT:
                        A(qT[:, :, tok(tt)], heads(bank(4 + tt % 2)), ACT.Copy, scale=float(DH) ** -0.5)
                    k0 = tt * P if tt < NS else (640 if tt == PROMPT else 512)
                    A(kT[:, k0:k0 + P], bank(6 + tt % 2, P), ACT.Copy).then_inc(qt_a.sem, 1)

                def exp_unit(u):
                    n = 640 if u // HQ < NS else P
                    w(act, mx_v, l, u + 1)
                    A(prob[u % 2][:, 0:n], two(2 * (u % 2))[:, 0:n], ACT.Exp, bias=negmax[:, u:u + 1],
                      accum_out=psums[:, u:u + 1]).then_inc(e_a.sem, 1)

                def take_att(tt):
                    w(act, at_p, l, tt + 1)
                    A(attT[:, :, tok(tt)], heads(bank(6 + tt % 2)), ACT.Copy).then_inc(at_a.sem, 1)

                NU = NT * HQ
                exp_unit(0)
                for u in range(NU):
                    w(act, pt_p, l, u + 1)
                    n = 640 if u // HQ < NS else P
                    A(probT[u % 2][:, 0:n], two(4)[:, 0:n], ACT.Copy).then_inc(pt_a.sem, 1)
                    if u + 1 < NU:
                        exp_unit(u + 1)
                    if u >= 12 and (u - 12) % HQ == 0:
                        take_att((u - 12) // HQ)
                take_att(NT - 1)
                A(sf_st[0], s_raw[:, 0:512], ACT.Copy).then_inc(st_a.sem, 1)
                A(sb_st[NS - 1], s_raw[:, 512:1024], ACT.Copy).then_inc(st_a.sem, 1)
                def take_ret(tt):
                    w(act, rt_p, l, tt + 1)
                    A(retT[:, :, tok(tt)], heads(bank(7)), ACT.Copy).then_inc(rt_ev.sem, 1)

                for tt in range(NT):
                    w(act, rk_p, l, tt + 1)
                    if tt >= 1:
                        w(act, in_p, l, tt)
                    A(flat(rkT), bank(3), ACT.Copy).then_inc(rk_a.sem, 1)
                    w(act, gr_p, l, tt + 1)
                    if tt >= 1:
                        w(act, rn_v, l, tt)
                    A(sgr, bank(5), ACT.Silu).then_inc(gr_a.sem, 1)
                    if tt >= 1:
                        take_ret(tt - 1)
                    root(bna[:, 0:4])
                take_ret(NT - 1)
                for g in range(2 * NT):
                    w(act, m_p, l, g + 1)
                    A((gu if g < NT else gv)[:, g % NT, :], bank(g % 4), ACT.Gelu_apprx_tanh).then_inc(m_a.sem, 1)
                root(st[:, 0:NT])
                for tt in range(NT):
                    w(act, cm_p, l, tt + 1)
                    A(cmT[:, :, tok(tt)], heads(bank(6 + tt % 2)), ACT.Copy).then_inc(cm_a.sem, 1)
                for n in range(24):
                    w(act, g_p, l, n + 1)
                    if n >= 2:
                        w(act, mix_v, l, n - 1)
                    A(sg[n % 2], two(2 * (n % 2)), ACT.Sigmoid).then_inc(g_a.sem, 1)
                w(act, x_v, l, 2 * NT)
                for tt in range(NT):
                    i = A(sq2, xr[:, tt, :], ACT.Square, accum_out=st[:, tt:tt + 1])
                    step.do(i) if tt < NT - 1 else i.then_inc(ssq2.sem, 1)
                root(st[:, 0:NT])
                for k in range(KD):
                    w(act, h2_p, l, k + 1)
                    A(h3[:, k, 0:512], bank(4 + k % 2), ACT.Copy).then_inc(h2_a.sem, 1)
                w(act, lo_p, l, 1)
                A(flat(r_sc), bank(0, NT * NE), ACT.Sigmoid).then_inc(sc_a.sem, 1)
                step.top_up()
                w_alone(act, tk_v, l, 1)

                def pair(j, n0):
                    def take_x(b):
                        act.wait_ge(xt_p.sem, xt_p.at(l, n0 + b + 1) + 2 * j)
                        A(xbT[b], ps[:, 0:2, :].rearrange("p b c -> p (b c)"), ACT.Copy).then_inc(xt_a.sem, 1)

                    def gate(b):
                        act.wait_ge(a_p.sem, a_p.at(l, 2 * (n0 + b) + 1) + 4 * j)
                        A(sa[b], bank(2 + b), ACT.Silu).then_inc(si_a.sem, 1)

                    def store(b):
                        act.wait_ge(y_out[b].sem, y_out[b].at(l, 16 * (n0 // 2)) + 16 * j)
                        for half in range(2):
                            act.wait_ge(y_p.sem, y_p.at(l, 2 * (n0 + b) + half + 1) + 4 * j)
                            A(yb[b][:, half * 512:half * 512 + 512], bank(7 - half), ACT.Copy).then_inc(y_a.sem, 1)
                        act.wait_ge(y_a.sem, y_a.at(l, 2 * (n0 + b) + 2) + 4 * j)
                        act.dma_start(y_dram[bass.ds((2 * j + (n0 + b)) * P, P), :], yb[b]).then_inc(y_out[b].sem, 16)

                    take_x(0)
                    gate(0)
                    take_x(1)
                    gate(1)
                    store(0)
                    store(1)

                with act.Fori(0, PAIRS) as j:
                    pair(j, 0)
                n_over = act.value_load(slots_u[0:1, N_OVER:N_OVER + 1], min_val=0, max_val=9)
                for b in range(2):
                    w_alone(act, y_out[b], l, 16 * PAIRS)
                with act.If(n_over > 0):
                    with act.Fori(0, OVER_PAIRS) as j:
                        pair(j, NE)
                with act.Else():
                    act.sem_inc(xt_a.sem, OVER)
                    act.sem_inc(si_a.sem, OVER)
                    act.sem_inc(y_a.sem, 2 * OVER)
                    for b in range(2):
                        act.sem_inc(y_out[b].sem, 16 * OVER_PAIRS)
                w_alone(act, x_new, l, 2)

        @block.vector
        def _(dve):
            V = dve
            TT, TS, STT = V.tensor_tensor, V.tensor_scalar, V.scalar_tensor_tensor
            V.wait_ge(const_in, 16 * 9)
            for l in range(LAYERS):
                for t in range(MODT):
                    n = l * MODT + t
                    V.wait_ge(mod_mm, n + 1)
                    if t == 0 and l > 0:
                        V.wait_ge(mod_st, 16 * l)
                    TT(out=mod_row[0:2, t * 512:(t + 1) * 512], in0=ps[0:2, n % 4, :],
                       in1=b_mod[l][0:2, t * 512:(t + 1) * 512], op=ALU.add).then_inc(mod_ev, 1)
                V.wait_ge(mod_ev, (l + 1) * MODT)
                for n, c in enumerate((1, 4)):
                    TS_ = mod_row[0:2, c * D:(c + 1) * D]
                    STT(out=TS_, in0=TS_, scalar=1.0, in1=norm_row[0:2, l, n, :], op0=ALU.add,
                        op1=ALU.mult).then_inc(mod_fold, 1)
            V.wait_ge(xin, 32)
            V.wait_ge(mod_st, 16 * LAYERS)
            V.sem_inc(x_new.sem, 1)
            V.sem_inc(y_a.sem, y_a.before)
            V.sem_inc(xt_p.sem, xt_p.before)
            for b in range(2):
                V.sem_inc(y_out[b].sem, y_out[b].before)

            with V.Fori(0, LAYERS) as l:
                step = Steps(V, v_step, l, waited)
                roots = [0]

                def inverse_root(ap, out, inv_n):
                    roots[0] += 1
                    TS(out=ap, in0=ap, scalar1=inv_n, scalar2=EPS, op0=ALU.mult, op1=ALU.add).then_inc(ms_v.sem, 1)
                    w(V, rt_a, l, roots[0])
                    step.do(V.reciprocal(out, ap))

                w(V, ssq1, l, 1)
                inverse_root(st[:, 0:NT], st2[:, 0:NT], 1.0 / D)
                for tt in range(NT):
                    TS(out=xn[:, tt, :], in0=xr[:, tt, :], scalar1=st2[:, tt:tt + 1], scalar2=None,
                       op0=ALU.mult).then_inc(xn_v.sem, 1)
                w(V, au_p, l, 1)
                V.tensor_copy(modc, bank(4, 32)).then_inc(mc_v.sem, 1)
                w(V, au_p, l, 2)
                V.tensor_copy(wsT, bank(5)).then_inc(ws_v.sem, 1)
                w(V, mc_v, l, 1)
                for k in range(KD):
                    w(V, tr_p, l, k + 1)
                    TS(out=h3[:, k, 512:640], in0=bank(2 + k % 2, P), scalar1=modc[:, 24 + k:25 + k],
                       scalar2=modc[:, 16 + k:17 + k], op0=ALU.mult, op1=ALU.add).then_inc(h_v.sem, 1)
                w(V, dec_a, l, 1)
                w(V, aux_in, l, aux_in.per)
                for f in range(2):
                    mask = dist[:, (2 * f + 1) * P:(2 * f + 2) * P].unsqueeze(1).broadcast_to([P, HR, P])
                    step.mark(TT(out=dec_tmp[:, f], in0=dec_tmp[:, f], in1=mask, op=ALU.mult))
                step.settle()
                TT(out=dec_in, in0=dec_tmp[:, 0], in1=dec_tmp[:, 1], op=ALU.add).then_inc(dec_v.sem, 1)
                w(V, dec_v, l, 1)

                for tt in range(NT):
                    w(V, z_a, l, NT + tt + 1)
                    step.do(TT(out=qk_tmp, in0=zq[:, tt, 0:640], in1=zq[:, tt, 0:640], op=ALU.mult))
                    step.do(V.tensor_reduce(st[:, tt * 10:tt * 10 + 10], qk_tmp.rearrange("p (h d) -> p h d", d=DH),
                                            AX.X, ALU.add))
                inverse_root(st[:, 0:50], st2[:, 0:50], 1.0 / DH)
                for tt in range(NT):
                    t10 = qk_tmp.rearrange("p (h d) -> p h d", d=DH)
                    z10 = zq[:, tt, 0:640].rearrange("p (h d) -> p h d", d=DH)
                    step.do(TT(out=t10, in0=z10, in1=st2[:, tt * 10:tt * 10 + 10].unsqueeze(2).broadcast_to([P, 10, DH]),
                               op=ALU.mult))
                    for half in range(2):
                        zz = zq[:, tt, 0:512].rearrange("p (i a d) -> p i a d", i=4, a=2)[:, :, half, :]
                        step.mark(TT(out=zz, in0=t10[:, 4 * half:4 * half + 4, :],
                                     in1=qk_gain[:, 0:DH].unsqueeze(1).broadcast_to([P, 4, DH]), op=ALU.mult))
                    i = TT(out=z10[:, 8:10, :], in0=t10[:, 8:10, :],
                           in1=qk_gain[:, DH:2 * DH].unsqueeze(1).broadcast_to([P, 2, DH]), op=ALU.mult)
                    if tt == PROMPT:
                        i.then_inc(qk_v.sem, 1)
                        continue
                    step.do(i)

                    def quarter(ap, b, n):
                        return ap.rearrange("p (h a b n) -> p h a b n", a=2, b=2, n=n)[:, :, :, b, :]

                    def rope(src, tmp, table, dim):
                        nh = src.shape[1] // dim
                        for b in range(2):
                            sin = quarter(table[:, tt, 1, :], b, dim // 4).broadcast_to([P, nh, 2, dim // 4])
                            step.mark(TT(out=quarter(tmp, b, dim // 4), in0=quarter(src, 1 - b, dim // 4), in1=sin,
                                         op=ALU.mult))
                        step.settle()
                        hh = src.rearrange("p (h d) -> p h d", d=dim)
                        step.do(TT(out=hh, in0=hh, in1=table[:, tt, 0, :].unsqueeze(1).broadcast_to([P, nh, dim]),
                                   op=ALU.mult))
                        return TT(out=src, in0=src, in1=tmp, op=ALU.add)

                    rope(zq[:, tt, 0:640], qk_tmp, rope_a, DH).then_inc(qk_v.sem, 1)
                    w(V, qk_v, l, tt + 1)
                for tt in range(NS):
                    w(V, z_a, l, 3 * NT + tt + 1)
                    rope(zr[:, tt, 0:2, :].rearrange("p i c -> p (i c)"), rope_tmp, rope_r, P).then_inc(rr_v.sem, 1)
                    w(V, rr_v, l, tt + 1)

                def att_out(tt):
                    w(V, pv_p, l, HQ * (tt + 1))
                    step.do(V.reciprocal(recip[:, HQ * tt:HQ * tt + HQ], psums[:, HQ * tt:HQ * tt + HQ]))
                    TT(out=zq[:, tt, 0:512].rearrange("p (h d) -> p h d", d=DH),
                       in0=bank(6 + tt % 2).rearrange("p (h d) -> p h d", d=DH),
                       in1=recip[:, HQ * tt:HQ * tt + HQ].unsqueeze(2).broadcast_to([P, HQ, DH]),
                       op=ALU.mult).then_inc(at_v.sem, 1)

                for u in range(NT * HQ):
                    w(V, s_p, l, u + 1)
                    n = 640 if u // HQ < NS else P
                    V.tensor_reduce(negmax[:, u:u + 1], two(2 * (u % 2))[:, 0:n], AX.X, ALU.max,
                                    negate=True).then_inc(mx_v.sem, 1)
                    if u >= 9 and (u - 9) % HQ == 0:
                        att_out((u - 9) // HQ)
                att_out(NT - 1)

                w(V, st_a, l, 2)
                for n, (back, tt) in enumerate(STATES):
                    w(V, kv_p, l, n + 1)
                    if tt == PROMPT:
                        V.tensor_copy(st_buf[back], bank(n % 2)).then_inc(kv_v.sem, 1)
                        continue
                    old, new = (sb_st[tt], sb_st[tt - 1]) if back else (sf_st[tt], sf_st[tt + 1])
                    step.do(TT(out=heads(st_tmp), in0=heads(old),
                               in1=dec_chunk[:, 4 * back:4 * back + 4].unsqueeze(2).broadcast_to([P, HR, P]),
                               op=ALU.mult))
                    TT(out=new, in0=st_tmp, in1=bank(n % 2), op=ALU.add).then_inc(kv_v.sem, 1)
                    w(V, kv_v, l, n + 1)
                w(V, kv_out, l, 32)
                for tt in range(NT):
                    w(V, rq_p, l, tt + 1)
                    if tt < NS:
                        step.mark(TT(out=rqTf, in0=heads(bank(2)), in1=dec_q[:, 0], op=ALU.mult))
                        step.mark(TT(out=rqTb, in0=heads(bank(2)), in1=dec_q[:, 1], op=ALU.mult))
                    V.tensor_copy(flat(rqT), bank(2)).then_inc(rq_v.sem, 1)
                    w(V, in_p, l, tt + 1)
                    TT(out=inner[tt % 2], in0=heads(bank(4)), in1=dec_in, op=ALU.mult).then_inc(in_v.sem, 1)
                    w(V, o_p, l, tt + 1)
                    for h in range(HR):
                        step.mark(V.bn_stats(bn[:, 6 * h:6 * h + 6], bank(6)[:, h * P:(h + 1) * P]))
                    step.settle()
                    for h in range(HR):
                        step.mark(V.bn_aggr(mean_var[:, 2 * h:2 * h + 2], bn[:, 6 * h:6 * h + 6]))
                    step.settle()
                    step.do(V.tensor_copy(bna[:, 0:4], mean_var[:, 1:8:2]))
                    inverse_root(bna[:, 0:4], bna[:, 4:8], 1.0)
                    for h in range(HR):
                        hs = slice(h * P, (h + 1) * P)
                        step.mark(TS(out=o_tmp[:, hs], in0=bank(6)[:, hs], scalar1=mean_var[:, 2 * h:2 * h + 1],
                                     scalar2=bna[:, 4 + h:5 + h], op0=ALU.subtract, op1=ALU.mult))
                    step.settle()
                    step.do(TT(out=o_tmp, in0=o_tmp, in1=ret_gain, op=ALU.mult))
                    w(V, gr_a, l, tt + 1)
                    TT(out=o_tmp, in0=o_tmp, in1=sgr, op=ALU.mult).then_inc(rn_v.sem, 1)
                for tt in range(NT):
                    w(V, m_a, l, NT + tt + 1)
                    step.do(V.tensor_tensor_reduce(mlp_tmp, gv[:, tt, :], gv[:, tt, :], 1.0, 0.0, ALU.mult, ALU.add,
                                                   st[:, tt:tt + 1]))
                inverse_root(st[:, 0:NT], st2[:, 0:NT], 1.0 / 512)
                for tt in range(NT):
                    STT(out=gv[:, tt, :], in0=gv[:, tt, :], scalar=st2[:, tt:tt + 1], in1=mlp_gain, op0=ALU.mult,
                        op1=ALU.mult).then_inc(vn_v.sem, 1)
                for tt in range(NT):
                    w(V, f_p, l, tt + 1)
                    for g in range(4):
                        gs = slice(g * P, (g + 1) * P)
                        i = STT(out=cmb[tt % 2][:, gs], in0=bank(4 + tt % 2)[:, gs], scalar=bs[:, g:g + 1],
                                in1=gu[:, tt, gs], op0=ALU.add, op1=ALU.mult)
                    i.then_inc(cm_v.sem, 1)
                w(V, st_out, l, 32)
                for n in range(24):
                    c = n % KD
                    w(V, g_a, l, n + 1)
                    w(V, o3_p, l, n + 1)
                    prod = two(4 + 2 * (n % 2))
                    if n < KD:
                        TT(out=mixT[:, c, :], in0=sg[n % 2], in1=prod, op=ALU.mult).then_inc(mix_v.sem, 1)
                    else:
                        w(V, mix_v, l, n)
                        step.do(TT(out=mix_tmp, in0=sg[n % 2], in1=prod, op=ALU.mult))
                        TT(out=mixT[:, c, :], in0=mixT[:, c, :], in1=mix_tmp, op=ALU.add).then_inc(mix_v.sem, 1)
                w(V, res_in, l, 48)
                for q in range(2 * NT):
                    half, tt = divmod(q, NT)
                    cs = slice(half * 512, half * 512 + 512)
                    w(V, w_p, l, q + 1)
                    if q >= 2:
                        w(V, x_v, l, q - 1)
                    step.do(TT(out=out_tmp[q % 2], in0=bank(q % 4), in1=gate1[:, cond_of(tt), cs], op=ALU.mult))
                    TT(out=xr[:, tt, cs], in0=xr[:, tt, cs], in1=out_tmp[q % 2], op=ALU.add).then_inc(x_v.sem, 1)
                w(V, ssq2, l, 1)
                inverse_root(st[:, 0:NT], st2[:, 0:NT], 1.0 / D)
                w(V, mod2_in, l, 64)
                for tt in range(NT):
                    step.do(STT(out=h2[:, tt, :], in0=xr[:, tt, :], scalar=st2[:, tt:tt + 1],
                                in1=gain2[:, cond_of(tt), :], op0=ALU.mult, op1=ALU.mult))
                    TT(out=h2[:, tt, :], in0=h2[:, tt, :], in1=shift2[:, cond_of(tt), :],
                       op=ALU.add).then_inc(h2_v.sem, 1)
                for k in range(KD):
                    w(V, h2_p, l, k + 1)
                    V.tensor_copy(h3[:, k, 512:640], bank(6 + k % 2, P)).then_inc(h2_q.sem, 1)

                def tiles_of(ap):
                    return ap.unsqueeze(1).broadcast_to([P, NT, NE])

                def per_tile(ap):
                    return ap.unsqueeze(2).broadcast_to([P, NT, NE])

                def dot(out, a, b):
                    step.do(TT(out=r_tmp, in0=a, in1=b, op=ALU.mult))
                    step.do(V.tensor_reduce(out, r_tmp, AX.X, ALU.add))

                w(V, sc_a, l, 1)
                step.mark(V.memset(r_gs, -BIG))
                step.do(TT(out=r_sel, in0=r_sc, in1=tiles_of(b_rt), op=ALU.add))
                s4 = [flat(r_sel)[:, e:NT * NE:EPG] for e in range(EPG)]
                step.mark(TT(out=r_m1, in0=s4[0], in1=s4[1], op=ALU.max))
                step.mark(TT(out=r_n1, in0=s4[0], in1=s4[1], op=ALU.min))
                step.mark(TT(out=r_m2, in0=s4[2], in1=s4[3], op=ALU.max))
                step.do(TT(out=r_n2, in0=s4[2], in1=s4[3], op=ALU.min))
                step.do(TT(out=r_n1, in0=r_n1, in1=r_n2, op=ALU.max))
                step.do(TT(out=r_n2, in0=r_m1, in1=r_m2, op=ALU.min))
                step.do(TT(out=r_m1, in0=r_m1, in1=r_m2, op=ALU.max))
                step.do(TT(out=r_n1, in0=r_n1, in1=r_n2, op=ALU.max))
                step.do(TT(out=r_gs[:, :, 0:NG], in0=r_m1.rearrange("p (t g) -> p t g", g=NG),
                           in1=r_n1.rearrange("p (t g) -> p t g", g=NG), op=ALU.add))
                for tt in range(NT):
                    step.do(V.max(r_top[:, tt, :], r_gs[:, tt, :]))
                    step.mark(V.max_index(r_gi[:, tt, :], r_top[:, tt, :], r_gs[:, tt, :]))
                step.settle()
                step.do(V.tensor_copy(r_gf, r_gi[:, :, 0]))
                step.do(TT(out=r_mask, in0=tiles_of(group_e), in1=per_tile(r_gf), op=ALU.is_equal))
                step.do(TS(out=r_mask, in0=r_mask, scalar1=-1.0, scalar2=BIG, op0=ALU.add, op1=ALU.mult))
                step.do(TT(out=r_masked, in0=r_sel, in1=r_mask, op=ALU.add))
                for tt in range(NT):
                    step.do(V.max(r_top[:, tt, :], r_masked[:, tt, :]))
                    step.mark(V.max_index(r_ei[:, tt, :], r_top[:, tt, :], r_masked[:, tt, :]))
                step.settle()
                for n in range(2):
                    step.do(V.tensor_copy(r_ef[n], r_ei[:, :, n]))
                    step.do(TT(out=(r_oh0, r_oh1)[n], in0=tiles_of(iota_e), in1=per_tile(r_ef[n]), op=ALU.is_equal))
                TT(out=r_oh, in0=r_oh0, in1=r_oh1, op=ALU.add).then_inc(oh_v.sem, 1)
                for n in range(2):
                    dot(r_w[n], r_sc, (r_oh0, r_oh1)[n])
                step.do(TT(out=r_sum, in0=r_w[0], in1=r_w[1], op=ALU.add))
                step.do(V.reciprocal(r_sum, r_sum))
                for n in range(2):
                    step.mark(TT(out=r_wn[n], in0=r_w[n], in1=r_sum, op=ALU.mult))
                w(V, rk_p2, l, 1)
                step.do(V.tensor_copy(r_cnt, ps[:, 1, 80:96]))
                step.do(TS(out=r_ov, in0=r_cnt, scalar1=full_blocks[:, 0:1], scalar2=None, op0=ALU.is_gt))
                for m in range(1, NT - 1):
                    step.do(STT(out=r_ov, in0=r_cnt, scalar=full_blocks[:, m:m + 1], in1=r_ov, op0=ALU.is_gt,
                                op1=ALU.add))
                step.do(V.tensor_copy(r_c0, r_ov))
                src, dst = r_c0, r_c1
                for sft in (1, 2, 4, 8):
                    step.mark(V.tensor_copy(dst[:, 0:sft], src[:, 0:sft]))
                    step.do(TT(out=dst[:, sft:NE], in0=src[:, sft:NE], in1=src[:, 0:NE - sft], op=ALU.add))
                    src, dst = dst, src
                run = src
                step.do(TT(out=r_ex, in0=run, in1=r_ov, op=ALU.subtract))
                step.do(TS(out=r_ex, in0=r_ex, scalar1=float(NE - 1), scalar2=None, op0=ALU.add))
                for n in range(2):
                    oh = (r_oh0, r_oh1)[n]
                    dot(r_rank[n], ps[:, 1, 0:80].rearrange("p (t e) -> p t e", e=NE), oh)
                    dot(r_ob, tiles_of(r_ex), oh)
                    step.mark(TS(out=r_hi, in0=r_rank[n], scalar1=float(P), scalar2=None, op0=ALU.is_ge))
                    step.do(TT(out=r_ob, in0=r_ob, in1=r_ef[n], op=ALU.subtract))
                    step.do(TT(out=r_hi, in0=r_hi, in1=r_ob, op=ALU.mult))
                    step.do(TT(out=r_hi, in0=r_hi, in1=r_ef[n], op=ALU.add))
                    step.do(STT(out=r_dest[n], in0=r_hi, scalar=float(P), in1=r_rank[n], op0=ALU.mult, op1=ALU.add))
                    step.do(V.tensor_copy(slots_u[:, DEST + NT * n:DEST + NT * n + NT], r_dest[n]))
                step.mark(V.tensor_copy(slots_u[:, N_OVER:N_OVER + 1], run[:, NE - 1:NE]))
                step.do(TT(out=r_le, in0=run.unsqueeze(1).broadcast_to([P, OVER, NE]),
                           in1=iota_b[:, 0:OVER].unsqueeze(2).broadcast_to([P, OVER, NE]), op=ALU.is_le))
                step.do(V.tensor_reduce(r_eo, r_le, AX.X, ALU.add))
                step.do(TS(out=r_eo, in0=r_eo, scalar1=float(NE - 1), scalar2=None, op0=ALU.min))
                V.tensor_copy(slots_u[:, E_OVER:E_OVER + OVER], r_eo).then_inc(de_v.sem, 1)
                w(V, tk_p, l, 1)
                V.tensor_copy(slots_u[:, 0:NBLK], ps[:, 2, 0:NBLK]).then_inc(tk_v.sem, 1)
                w_alone(V, tk_v, l, 1)

                def pair(j, n0):
                    for b in range(2):
                        V.wait_ge(si_a.sem, si_a.at(l, n0 + b + 1) + 2 * j)
                        V.wait_ge(a_p.sem, a_p.at(l, 2 * (n0 + b) + 2) + 4 * j)
                        TT(out=hd[b], in0=sa[b], in1=bank(4 + b), op=ALU.mult).then_inc(hd_v.sem, 1)
                        V.wait_ge(ht_p.sem, ht_p.at(l, n0 + b + 1) + 2 * j)
                        V.tensor_copy(hdT[b], bank(6)).then_inc(ht_v.sem, 1)

                with V.Fori(0, PAIRS) as j:
                    pair(j, 0)
                n_over = V.value_load(slots_u[0:1, N_OVER:N_OVER + 1], min_val=0, max_val=9)
                w(V, hd_v, l, NE)
                w_alone(V, ht_v, l, NE)
                with V.If(n_over > 0):
                    with V.Fori(0, OVER_PAIRS) as j:
                        pair(j, NE)
                with V.Else():
                    V.sem_inc(hd_v.sem, OVER)
                    V.sem_inc(ht_v.sem, OVER)
                w(V, cx_in, l, 16)
                w(V, g2_in, l, 32)
                for tt in range(NT):
                    b = tt % 2
                    w(V, y1_in[b], l, 16 * (tt // 2 + 1))
                    w(V, y2_in[b], l, 16 * (tt // 2 + 1))
                    if tt >= 1:
                        w(V, cb_v, l, tt)
                    step.do(TS(out=cb_tmp, in0=y1[b], scalar1=r_wn[0][:, tt:tt + 1], scalar2=None, op0=ALU.mult))
                    step.do(STT(out=cb_tmp, in0=y2[b], scalar=r_wn[1][:, tt:tt + 1], in1=cb_tmp, op0=ALU.mult,
                                op1=ALU.add))
                    step.do(TT(out=cb_tmp, in0=cb_tmp, in1=gate2[:, cond_of(tt), :], op=ALU.mult))
                    TT(out=xr[:, tt, :], in0=xr[:, tt, :], in1=cb_tmp, op=ALU.add).then_inc(cb_v.sem, 1)
                w(V, cb_v, l, NT)
                step.top_up()
                V.sem_inc(x_new.sem, 1)

        @block.gpsimd
        def _(pool):
            G = pool
            G.dma_start(const[:, :], I["persistent"]).then_inc(const_in, 16)
            for n, nm in enumerate(("norm1", "norm2")):
                G.dma_start(norm_row[0:2, :, n, :], I[nm].partition_broadcast(2)).then_inc(const_in, 16)
            for n, nm in enumerate(("c", "c_ctx")):
                src = I[nm].rearrange("o (k p) -> (o k) p", p=P) if nm == "c" else I[nm].rearrange("(k p) -> k p", p=P)
                G.dma_start(cond_rows[KD * n:KD * n + KD, :], src).then_inc(const_in, 16)
            for n in range(LAYERS):
                G.dma_start(b_mod[n][0:2, :], I["b_mod"][n].partition_broadcast(2)).then_inc(const_in, 16)
            G.dma_start(w_rt.rearrange("p (k e) -> p k e", k=KD),
                        I["w_router"].rearrange("(k p) e -> p k e", p=P)).then_inc(const_in, 16)
            G.dma_start(b_rt, I["b_router"].partition_broadcast(P)).then_inc(const_in, 16)
            G.dma_start(xr[:, 0:NS, :], I["x_sample"].rearrange("o (t p) d -> p (o t) d", p=P)).then_inc(xin, 16)
            G.dma_start(xr[:, PROMPT, :], I["x_prompt"].rearrange("o p d -> (o p) d")).then_inc(xin, 16)
            G.memset(zeros, 0.0).then_inc(zeroed, 1)
            G.wait_ge(zeroed, 1)
            G.dma_start(tok_dram.rearrange("(b p) o -> b (p o)", p=P), zeros[0:NBLK, 0:P]).then_inc(tok_zero, 16)
            for half in range(2):
                G.dma_start(y_dram[NE * P:NBLK * P, half * 512:half * 512 + 512].rearrange("(b p) d -> p b d", p=P),
                            zeros.unsqueeze(1).broadcast_to([P, OVER, 512])).then_inc(tok_zero, 16)
            for n in range(LAYERS):
                G.wait_ge(mod_fold, 2 * (n + 1))
                G.dma_start(mod_dram[n].rearrange("s m d -> s (m d)"), mod_row[0:2, :]).then_inc(mod_st, 16)
            G.wait_ge(mod_st, 16 * LAYERS)
            G.wait_ge(tok_zero, 48)

            with G.Fori(0, LAYERS) as l:
                def dyn(ap):
                    return ap[bass.ds(l, 1)]

                def spread(out, ap):
                    return G.dma_start(out, ap.partition_broadcast(P))

                def mod_row_of(cond, m):
                    return dyn(mod_dram)[:, cond, m, :].rearrange("o d -> (o d)")

                for cond in range(2):
                    G.dma_start(mod_rows[2 * KD * cond:2 * KD * cond + 2 * KD, :],
                                dyn(mod_dram)[:, cond, 0:2, :].rearrange("o m (k p) -> (o m k) p", p=P)
                                ).then_inc(aux_in.sem, 16)
                for out, nm in ((qk_gain[:, 0:DH], "q_norm"), (qk_gain[:, DH:2 * DH], "k_norm"),
                                (ret_gain, "ret_gn"), (mlp_gain, "mlp_norm"), (lg[:, 0:4], "ret_decay_fwd"),
                                (lg[:, 4:8], "ret_decay_bwd")):
                    spread(out, dyn(I[nm]).rearrange("o d -> (o d)")).then_inc(aux_in.sem, 16)
                G.dma_start(ws_raw.rearrange("p (g j) -> p g j", g=4),
                            dyn(I["w_spatial"]).rearrange("o g i j -> i (o g) j")).then_inc(aux_in.sem, 16)
                with nc.allow_non_contiguous_dma(reason="512 numbers, once per layer"):
                    G.dma_start(bs, dyn(I["b_spatial"]).rearrange("o g i -> i (o g)")).then_inc(aux_in.sem, 16)
                G.dma_start(kc_raw, I["cache_k"][:, bass.ds(l, 1)].rearrange("b o t h d -> (b o t) (h d)")
                            ).then_inc(aux_in.sem, 16)
                G.dma_start(v_cache, I["cache_v"][:, bass.ds(l, 1)].rearrange("b o t h d -> (b o t) (h d)")
                            ).then_inc(aux_in.sem, 16)
                for n, nm in enumerate(("state_ret_fwd", "state_ret_bwd")):
                    G.dma_start(heads(s_raw[:, 512 * n:512 * n + 512]),
                                I[nm][:, bass.ds(l, 1)].rearrange("b o h d e -> d (b o h) e")).then_inc(aux_in.sem, 16)
                G.dma_start(dist, I["distances"]).then_inc(aux_in.sem, 16)
                w(G, x_new, l, 1)
                G.dma_start(x_dram.rearrange("(t p) d -> p t d", p=P), xr).then_inc(xs_out.sem, 16)
                w(G, qk_v, l, NT)
                w(G, z_a, l, 2 * NT)
                for n, nm in enumerate(("new_k", "new_v")):
                    G.dma_start(O[nm][:, bass.ds(l, 1)].rearrange("b o t h d -> (b o t) (h d)"),
                                zq[:, PROMPT, 512 + P * n:640 + P * n]).then_inc(kv_out.sem, 16)
                w(G, rr_v, l, NS)
                w(G, z_a, l, 5 * NT)
                w(G, dec_a, l, 1)
                w(G, s_p, l, NT * HQ)
                w(G, qt_a, l, NT + 1)
                for n, (back, tt) in enumerate(STATES):
                    if n >= 2:
                        w(G, kv_p, l, n - 1)
                    G.tensor_tensor(out=heads(kdec[n % 2]), in0=heads(zr[:, tt, 1, :]),
                                    in1=dec_k[:, 4 * back:4 * back + 4].unsqueeze(2).broadcast_to([P, HR, P]),
                                    op=ALU.mult).then_inc(kd_g.sem, 1)
                for back, nm in enumerate(("new_sf", "new_sb")):
                    w(G, kv_v, l, 7 + back)
                    G.dma_start(O[nm][:, bass.ds(l, 1)].rearrange("b o h d e -> d (b o h) e"),
                                heads(st_buf[back])).then_inc(st_out.sem, 16)
                w(G, xs_out, l, 16)
                w(G, cm_v, l, NT)
                G.dma_start(xr, x_dram.rearrange("(t p) d -> p t d", p=P)).then_inc(res_in.sem, 16)
                for cond in range(2):
                    spread(gate1[:, cond, :], mod_row_of(cond, 2)).then_inc(res_in.sem, 16)
                w(G, x_v, l, 2 * NT)
                for cond in range(2):
                    spread(shift2[:, cond, :], mod_row_of(cond, 3)).then_inc(mod2_in.sem, 16)
                    spread(gain2[:, cond, :], mod_row_of(cond, 4)).then_inc(mod2_in.sem, 16)
                G.dma_start(x_dram.rearrange("(t p) d -> p t d", p=P), xr).then_inc(xm_out.sem, 16)
                w(G, h2_v, l, NT)
                G.dma_start(h2_dram.rearrange("(t p) d -> p t d", p=P), h2).then_inc(h2_out.sem, 16)
                w(G, de_v, l, 1)
                for n in range(2):
                    for tt in range(NT):
                        c = DEST + NT * n + tt
                        G.indirect_dma_start(tok_dram, bass.IndirectOffsetOnAxis(ap=slots_u[:, c:c + 1], axis=0),
                                             token_id[:, tt:tt + 1], None).then_inc(tok_out.sem, 16)
                w(G, tok_out, l, tok_out.per)
                G.dma_start(r_tok[0:NBLK, :], tok_dram.rearrange("(b p) o -> b (p o)", p=P)).then_inc(tok_in.sem, 16)
                w(G, tk_v, l, 1)
                w(G, h2_out, l, 16)

                def pair(j, n0):
                    for b in range(2):
                        G.wait_ge(xt_p.sem, xt_p.at(l, n0 + b - 1) + 2 * j)
                        G.sem_inc(waited, 1)
                        G.tensor_copy(slots_u[:, BLK_IDX + b:BLK_IDX + b + 1],
                                      slots_u[:, bass.ds(2 * j + (n0 + b), 1)]).then_inc(idx_g.sem, 1)
                        G.wait_ge(idx_g.sem, idx_g.at(l, n0 + b + 1) + 2 * j)
                        G.sem_inc(waited, 1)
                        G.indirect_dma_start(xb[b], None, h2_dram,
                                             bass.IndirectOffsetOnAxis(ap=slots_u[:, BLK_IDX + b:BLK_IDX + b + 1], axis=0)
                                             ).then_inc(xb_in[b].sem, 16)

                with G.Fori(0, PAIRS) as j:
                    pair(j, 0)
                n_over = G.value_load(slots_u[0:1, N_OVER:N_OVER + 1], min_val=0, max_val=9)
                w(G, idx_g, l, NE)
                w(G, xt_p, l, NE)
                for b in range(2):
                    w(G, xb_in[b], l, 16 * PAIRS)
                with G.If(n_over > 0):
                    with G.Fori(0, OVER_PAIRS) as j:
                        pair(j, NE)
                with G.Else():
                    G.sem_inc(idx_g.sem, OVER)
                    for b in range(2):
                        G.dma_start(xb[b][0:16, 0:16], h2_dram[0:16, 0:16]).then_inc(xb_in[b].sem, 16 * OVER_PAIRS)
                for b in range(2):
                    w(G, xb_in[b], l, xb_in[b].per)
                w(G, y_p, l, 2 * NB2)
                w(G, xm_out, l, 16)
                G.dma_start(xr, x_dram.rearrange("(t p) d -> p t d", p=P)).then_inc(cx_in.sem, 16)
                for cond in range(2):
                    spread(gate2[:, cond, :], mod_row_of(cond, 5)).then_inc(g2_in.sem, 16)
                for b in range(2):
                    w(G, y_out[b], l, y_out[b].per)
                for tt in range(NT):
                    b = tt % 2
                    if tt >= 2:
                        w(G, cb_v, l, tt - 1)
                    for n, (dst, sig) in enumerate(((y1[b], y1_in[b]), (y2[b], y2_in[b]))):
                        c = DEST + NT * n + tt
                        G.indirect_dma_start(dst, None, y_dram, bass.IndirectOffsetOnAxis(ap=slots_u[:, c:c + 1], axis=0)
                                             ).then_inc(sig.sem, 16)
                w_alone(G, x_new, l, 2)
            G.dma_start(O["y_sample"].rearrange("o (t p) d -> p (o t) d", p=P), xr[:, 0:NS, :]).then_inc(fin_out, 16)
            G.dma_start(O["y_prompt"].rearrange("o p d -> (o p) d"), xr[:, PROMPT, :]).then_inc(fin_out, 16)
            G.wait_ge(kv_out.sem, LAYERS * kv_out.per)
            G.wait_ge(st_out.sem, LAYERS * st_out.per)
            G.wait_ge(fin_out, 32)


_INS = ["x_prompt", "x_sample", "cache_k", "cache_v", "state_ret_fwd", "state_ret_bwd", "c", "c_ctx", "w_mod", "b_mod",
        "norm1", "norm2", "w_in", "q_norm", "k_norm", "ret_decay_fwd", "ret_decay_bwd", "ret_gn", "mlp_norm",
        "w_spatial", "b_spatial", "w_att_o", "w_ret_o", "w_mlp_o", "w_out", "w_router", "b_router", "w_gate", "w_up",
        "w_down"]
_OUTS = [("y_prompt", (1, P, D)), ("y_sample", (1, NS * P, D)), ("new_k", (1, LAYERS, P, HKV, DH)),
         ("new_v", (1, LAYERS, P, HKV, DH)), ("new_sf", (1, LAYERS, HR, P, P)), ("new_sb", (1, LAYERS, HR, P, P))]


def kernel(**inputs):
    import numpy as _np
    import concourse.bacc as _bacc
    from concourse import mybir as _mybir
    from concourse.bass_utils import run_bass_kernel_spmd as _run

    nc = _bacc.Bacc("TRN2", target_bir_lowering=False, num_devices=1)
    arrays, ins, outs = {}, {}, {}
    for name in _INS:
        a = _np.ascontiguousarray(inputs[name])
        arrays[f"in_{name}_dram"] = a
    arrays["in_persistent_dram"] = PERSISTENT
    arrays["in_distances_dram"] = DISTANCES
    for key, a in arrays.items():
        ins[key[3:-5]] = nc.dram_tensor(key, a.shape, _mybir.dt.from_np(a.dtype), kind="ExternalInput").ap()
    for i, (name, shape) in enumerate(_OUTS):
        outs[name] = nc.dram_tensor(f"out_{i}_dram", shape, _mybir.dt.float32, kind="ExternalOutput").ap()
    trunk(nc, ins, outs)
    r = _run(nc, [arrays], core_ids=[0])
    return tuple(r.results[0][f"out_{i}_dram"] for i in range(len(_OUTS)))
```

```python
from contextlib import ExitStack

import numpy as np

import concourse.bass as bass
from concourse import mybir

F32 = mybir.dt.float32
U32 = mybir.dt.uint32
F32R = mybir.dt.float32r
ALU = mybir.AluOpType
ACT = mybir.ActivationFunctionType
AX = mybir.AxisListType

P = 128
D = 1024
KD = D // P
LAYERS = 2
NT = 5
NS = 4
PROMPT = NT - 1
T = NT * P
GRID_W = 64
EPS = 1e-6
HQ, HKV, DH = 8, 2, 64
HR = 4
NMOD = 6
IN_COLS = 6912
C_QR, C_MU, C_GATE = 768, 2816, 3840
NE, NG, EPG = 16, 4, 4
FF = 512
NBLK = 26
NTAB = NBLK + 2
PAIRS = NE // 2
OVER_PAIRS = (NBLK - NE) // 2
SLOT = 4096
BIG = 1.0e30
QK_TURNS = ((0,), (1, 2), (3,), (4, 5))
DEST, N_OVER, E_OVER = NTAB, NTAB + 2 * NT, NTAB + 2 * NT + 1
OVER = 2 * OVER_PAIRS
BLK_IDX = E_OVER + OVER
STATES = [(0, 0), (0, 1), (0, 2), (1, 3), (1, 2), (1, 1), (0, PROMPT), (1, PROMPT)]


def rope_table(dim):
    rows = NS * P // GRID_W
    r = np.repeat(np.arange(rows, dtype=np.float32), GRID_W)
    c = np.tile(np.arange(GRID_W, dtype=np.float32), rows)
    half = dim // 2
    inv = np.float32(10000.0) ** (-np.arange(0, half, 2, dtype=np.float32) / np.float32(half))
    ar, ac = r[:, None] * inv, c[:, None] * inv
    ang = np.concatenate([ar, ar, ac, ac], axis=-1).astype(np.float64)
    sign = np.tile(np.repeat([-1.0, 1.0], dim // 4), 2)
    both = np.stack([np.cos(ang), np.sin(ang) * sign], axis=1).astype(np.float32)
    return both.reshape(NS, P, 2 * dim).transpose(1, 0, 2).reshape(P, -1)


def shape_tables():
    i = np.arange(P, dtype=np.float32)
    row = np.broadcast_to(i, (P, P))
    col = row.T
    persistent = [np.eye(P), (col < row), np.ones((P, P)), rope_table(DH), rope_table(P),
                  np.stack([P - 1 - i, i], 1), np.broadcast_to(np.arange(NE), (P, NE)),
                  np.broadcast_to(np.arange(NE) // EPG, (P, NE)),
                  i[:, None] + P * np.arange(NT)[None, :],
                  np.broadcast_to(P * np.arange(1, NT), (P, NT - 1)),
                  np.broadcast_to(np.arange(NTAB), (P, NTAB)), row]
    distances = [np.maximum(row - col, 0), (row >= col), np.maximum(col - row, 0), (col >= row),
                 row + 1, P - row]
    return (np.concatenate(persistent, 1).astype(np.float32),
            np.concatenate(distances, 1).astype(np.float32))


PERSISTENT, DISTANCES = shape_tables()


class Signal:

    def __init__(self, sem, per, before=0):
        self.sem, self.per, self.before = sem, per, before

    def at(self, l, n):
        return l * self.per + (self.before + n)


class Steps:

    def __init__(self, eng, sem):
        self.eng, self.sem, self.n = eng, sem, 0

    def mark(self, ins):
        ins.then_inc(self.sem, 1)
        self.n += 1

    def settle(self):
        self.eng.wait_ge(self.sem, self.n)

    def do(self, ins):
        self.mark(ins)
        self.settle()


def trunk(nc, I, O):
    with ExitStack() as ctx:
        def sem(name):
            return ctx.enter_context(nc.semaphore(name))

        def signal(name, per, before=0):
            return Signal(sem(name), per, before)

        def sb(name, cols, dt=F32):
            return ctx.enter_context(nc.sbuf_tensor(name, [P, cols], dt))

        mod_dram = nc.dram_tensor("mod_dram", (LAYERS, 2, NMOD, D), F32, kind="Internal").ap()
        x_dram = nc.dram_tensor("x_dram", (T, D), F32, kind="Internal").ap()
        h2_dram = nc.dram_tensor("h2_dram", (T, D), F32, kind="Internal").ap()
        y_dram = nc.dram_tensor("y_dram", (NBLK * P, D), F32, kind="Internal").ap()

        base = -(-nc.sbuf_base // 32) * 32
        ring_lo = sb("ring_lo", 4 * SLOT)
        work = sb("work", 17664)
        hT = sb("hT", KD * T)
        branch = sb("branch", 3 * 4 * T)
        const = sb("const", PERSISTENT.shape[1])
        small = sb("small", 3900)
        slots_u = sb("slots_u", BLK_IDX + 2, U32)

        def rounded(name, column, cols):
            return nc.alloc_sbuf_tensor_at(name, [P, cols], F32R, offset=base + 4 * column)[:, :]

        slot_r = [rounded(f"slot{s}_rounded", s * SLOT, SLOT) for s in range(4)]
        h_hi = rounded("h_hi", 4 * SLOT, KD * T)
        w_hi = [rounded(f"w_hi{b}", 4 * SLOT + KD * T + b * D, D) for b in range(3)]
        h_lo = rounded("h_lo", 4 * SLOT + 17664, KD * T)
        after_h = 4 * SLOT + 17664 + KD * T
        h_high = [rounded(f"h_high{i}", after_h + 8 * T * i, 4 * T) for i in range(2)]
        ps = ctx.enter_context(nc.psum_tensor("ps", [P, 8, 512], F32))

        def w_(a, n):
            return work[:, a:a + n]

        slot = [ring_lo[:, s * SLOT:(s + 1) * SLOT] for s in range(4)] + [w_(0, SLOT), w_(SLOT, SLOT)]

        at = [0]

        def take(tensor, n):
            at[0] += n
            return tensor[:, at[0] - n:at[0]]

        ident = take(const, P)
        before = take(const, P)
        ones = take(const, P)
        rope_a = take(const, NS * 2 * DH).rearrange("p (t s d) -> p t s d", t=NS, s=2)
        rope_r = take(const, NS * 2 * P).rearrange("p (t s d) -> p t s d", t=NS, s=2)
        kpos = take(const, 2)
        iota_e = take(const, NE)
        group_e = take(const, NE)
        token_id = take(const, NT)
        full_blocks = take(const, NT - 1)
        iota_b = take(const, NTAB)
        iota_s = take(const, P)
        assert at[0] == PERSISTENT.shape[1]
        at[0] = 0
        dec_q = take(small, 2 * HR * P).rearrange("p (f h i) -> p f h i", f=2, h=HR)
        dec_in = take(small, HR * P).rearrange("p (h i) -> p h i", h=HR)
        dec_k = take(small, 2 * HR)
        dec_chunk = take(small, 2 * HR)
        lg = take(small, 2 * HR)
        qk_gain = take(small, 2 * DH)
        ret_gain = take(small, 512)
        mlp_gain = take(small, 512)
        wsT = take(small, 4 * P)
        bs = take(small, 4)
        modc = take(small, 40)
        w_rt = take(small, KD * NE)
        b_rt = take(small, NE)
        st = take(small, 60)
        st2 = take(small, 60)
        bn = take(small, HR * 6)
        bna = take(small, HR * 2)
        negmax = take(small, 40)
        psums = take(small, 40)
        recip = take(small, 40)
        scT = take(small, 16)
        mean_var = take(small, 2 * HR)
        v_cache = take(small, P)
        assert at[0] <= 3900, at[0]

        xr = w_(0, NT * D).rearrange("p (t d) -> p t d", t=NT)
        attT = branch[:, 0:4 * T].rearrange("p (c t) -> p c t", c=4)
        retT = branch[:, 4 * T:8 * T].rearrange("p (c t) -> p c t", c=4)
        cmT = branch[:, 8 * T:12 * T].rearrange("p (c t) -> p c t", c=4)
        aux = branch[:, 4 * T:8 * T]
        dist = aux[:, 0:6 * P]
        ws_raw = aux[:, 768:1280]
        mod_rows = aux[0:40, 1280:1408]
        kc_raw = aux[:, 1408:1536]
        s_raw = aux[:, 1536:2560]
        h3 = hT[:, :].rearrange("p (k t) -> p k t", k=KD)

        const_in = sem("const_in")
        xin = sem("xin")
        cond_t = sem("cond_t")
        cond_s = sem("cond_s")
        mod_mm = sem("mod_mm")
        mod_ev = sem("mod_ev")
        mod_st = sem("mod_st")
        zeroed = sem("zeroed")
        y_zero = sem("y_zero")
        cond_in = sem("cond_in")
        bias_in = sem("bias_in")
        waited = sem("waited")

        MODT = 2 * NMOD
        MOD_A = 8
        mixer = [("q", 0), ("kv", 1), ("qr", 2), ("kr", 0), ("vr", 2), ("gr", 0), ("mu", 1), ("mv", 3),
                 ("o0", 2), ("g00", 1), ("g01", 0), ("o1", 3), ("g10", 1), ("g11", 0),
                 ("o2", 2), ("g20", 1), ("g21", 0), ("out0", 3), ("out1", 1)]
        high_slot = {"qr": 3, "kr": 1, "vr": 3}
        guest = {"mu": "kr", "mv": "vr"}
        uses, use_of, slot_of, plan, expert_base = [0] * 6, {}, {}, [], {}

        def planned(key, s):
            use_of[key], slot_of[key] = uses[s], s
            uses[s] += 1
            plan.append(key)

        for t in range(MODT):
            planned(("mod", 0, t), t % 4)
        for l in range(LAYERS):
            for name, s in mixer:
                planned((l, name), s)
            if l + 1 < LAYERS:
                for t in range(MOD_A):
                    planned(("mod", l + 1, t), (0, 2, 3, 1, 0, 1, 3, 2)[t])
            expert_base[l] = list(uses)
            plan.append(("experts", l))
            uses = [u + PAIRS + OVER_PAIRS for u in uses]
            if l + 1 < LAYERS:
                for t in range(MOD_A, MODT):
                    planned(("mod", l + 1, t), (t - MOD_A) % 4)
        full = [sem(f"slot{s}_full") for s in range(6)]

        aux_in = signal("aux_in", 16 * 14)
        modr_in = signal("mod_rows_in", 32)
        xs_out = signal("xs_out", 16)
        v_step = sem("dve_step")
        a_step = sem("act_step")
        ssq1 = signal("ssq1", NT)
        rt_a = signal("roots", 17)
        ms_v = signal("mean_squares", 17)
        xn_v = signal("xn_ready", NT)
        tr_p = signal("xn_turned", NT)
        h_a = signal("h_low", NT)
        h_v = signal("h_high", NT)
        au_p = signal("aux_turned", 2)
        mc_v = signal("mod_cols", 2)
        ws_v = signal("ws_ready", 1)
        dec_a = signal("decays_exp", 1)
        dec_v = signal("decays_ready", 1)
        hs_v = signal("h_split", NT)
        zh_v = signal("z_high_parts", 3)
        zl_g = signal("z_low_parts", 3)
        hr_g = signal("h_joined", 2)
        z_p = signal("z_product", 25)
        z_a = signal("z_taken", 25)
        qk_v = signal("qk_ready", NT)
        kv_out = signal("kv_out", 32)
        rr_v = signal("ret_roped", NS)
        qt_p = signal("qk_turned", 6)
        qt_a = signal("qkT_ready", 6)
        s_p = signal("scores", 40)
        mx_v = signal("max_ready", 40)
        e_a = signal("probs", 40)
        pt_p = signal("probs_turned", 40)
        pt_a = signal("probsT_ready", 40)
        pv_p = signal("pv_done", 40)
        at_v = signal("att_ready", NT)
        at_p = signal("att_turned", NT)
        at_a = signal("attT_ready", NT)
        kd_g = signal("kdec_ready", 8)
        kv_p = signal("kv_product", 8)
        kv_v = signal("state_ready", 8)
        st_a = signal("start_states", 2)
        st_out = signal("state_out", 32)
        rq_p = signal("ret_q_turned", NT)
        rk_p = signal("ret_k_turned", NT)
        rq_v = signal("ret_qT", NT)
        rk_a = signal("ret_kT", NT)
        in_p = signal("inner_product", NT)
        in_v = signal("inner_ready", NT)
        gr_p = signal("gr_product", NT)
        gr_a = signal("gr_silu", NT)
        o_p = signal("ret_out", NT)
        rn_v = signal("ret_normed", NT)
        rt_p = signal("ret_turned", NT)
        rt_ev = signal("retT_ready", NT)
        m_p = signal("mlp_product", 10)
        m_a = signal("mlp_gelu", 10)
        vn_v = signal("mlp_normed", NT)
        f_p = signal("spatial", NT)
        cm_v = signal("cm_ready", NT)
        cm_p = signal("cm_turned", NT)
        cm_a = signal("cmT_ready", NT)
        hh_v = signal("h_high_parts", 1)
        hl_g = signal("h_low_parts", 2)
        wg_v = signal("gate_split", 24)
        g_p = signal("gate_product", 24)
        g_a = signal("gate_sigmoid", 24)
        o3_p = signal("branch_product", 24)
        mix_v = signal("mix_ready", 24)
        res_in = signal("residual_in", 48)
        w_p = signal("out_product", 10)
        x_v = signal("x_mid", 10)
        mod2_in = signal("mod2_in", 16 * 3)
        mod2p_in = signal("mod2p_in", 32)
        ssq2 = signal("ssq2", NT)
        h2_v = signal("h2_ready", NT)
        h2_out = signal("h2_out", 16 * NT)
        h2_p = signal("h2_turned", NT)
        h2_a = signal("h2T_low", NT)
        h2_q = signal("h2T_high", NT)
        lo_p = signal("logits", 1)
        sc_a = signal("scores_ready", 1)
        oh_v = signal("one_hots", 1)
        rk_p2 = signal("ranks", 1)
        de_v = signal("dest_ready", 1)
        tab_v = signal("slot_one_hots", 2)
        tk_p = signal("token_table", 1)
        tk_v = signal("tok_ready", 1)
        NB2 = 2 * (PAIRS + OVER_PAIRS)
        idx_g = signal("block_idx", NB2 + 1)
        xb_in = [signal(f"xb_in{b}", 16 * (NB2 // 2 + 1 - b)) for b in range(2)]
        xt_p = signal("xb_turned", NB2 + 1)
        xt_a = signal("xbT_ready", NB2 + 1)
        a_p = signal("gate_up", 2 * NB2)
        si_a = signal("silu_gate", NB2)
        hd_v = signal("hidden", NB2)
        ht_p = signal("hidden_turned", NB2)
        ht_v = signal("hiddenT", NB2)
        y_p = signal("down", 2 * NB2)
        y_a = signal("y_ready", 2 * NB2, 3)
        y_out = [signal(f"y_out{b}", 16 * NB2 // 2, 16) for b in range(2)]
        w0_a = signal("y1_weighted", NT)
        g2_in = signal("gate2_in", 32)
        y1_in = [signal(f"y1_in{b}", 16 * (3 if b == 0 else 2)) for b in range(2)]
        y2_in = [signal(f"y2_in{b}", 16 * (3 if b == 0 else 2)) for b in range(2)]
        cb_v = signal("combined", NT)
        fin_out = sem("fin_out")

        def w(eng, sig, l, n):
            eng.wait_ge(sig.sem, sig.at(l, n))

        def w_loop(eng, sig, value):
            eng.wait_ge(sig.sem, value)
            eng.sem_inc(waited, 1)

        def full_at(key):
            return 16 * (use_of[key] + 1)

        def last_read(key):
            if key[0] == "mod":
                return mod_mm, MODT * key[1] + key[2] + 1
            l, name = key
            z = {"q": (z_p, 2 * NT - 1), "kv": (z_p, 2 * NT), "qr": (z_p, 3 * NT), "kr": (z_p, 4 * NT),
                 "vr": (z_p, 5 * NT), "gr": (gr_p, NT), "mu": (m_p, NT), "mv": (m_p, 2 * NT),
                 "out0": (w_p, 2 * NT - 1), "out1": (w_p, 2 * NT)}
            for b in range(3):
                z[f"g{b}0"] = (g_p, 8 * b + 4)
                z[f"g{b}1"] = (g_p, 8 * b + 8)
                z[f"o{b}"] = (o3_p, 8 * b + 8)
            sig, n = z[name]
            return sig.sem, sig.at(l, n)

        block = ctx.enter_context(nc.Block())

        @block.sync
        def _(sp):
            def load(s, src, nk, cols):
                sp.dma_start(slot[s][:, 0:nk * cols].rearrange("p (k c) -> p k c", k=nk), src).then_inc(full[s], 16)

            def rows(ap):
                return ap.rearrange("(k p) c -> p k c", p=P)

            def source(key):
                if key[0] == "mod":
                    return rows(I["w_mod"][key[1], :, key[2] * 512:(key[2] + 1) * 512]), KD, 512
                l, name = key
                if name[0] == "o" and name[1] != "u":
                    return rows(I[("w_att_o", "w_ret_o", "w_mlp_o")[int(name[1])]][l]), 4, D
                if name[:3] == "out":
                    h = int(name[3])
                    return rows(I["w_out"][l, :, 512 * h:512 * h + 512]), KD, 512
                c0 = {"q": 0, "kv": 512, "qr": C_QR, "kr": C_QR + 512, "vr": C_QR + 1024, "gr": C_QR + 1536,
                      "mu": C_MU, "mv": C_MU + 512}.get(name)
                if c0 is None:
                    c0 = C_GATE + D * int(name[1]) + 512 * int(name[2])
                cols = 256 if name == "kv" else 512
                return rows(I["w_in"][l, :, c0:c0 + cols]), KD, cols

            def expert(l, e, half):
                for i, (nm, nk, cols) in enumerate((("w_gate", KD, FF), ("w_up", KD, FF), ("w_down", 4, D))):
                    src = I[nm][l:l + 1, bass.ds(e, 1)].rearrange("o e (k p) c -> p (o e k) c", p=P)
                    yield 3 * half + i, src, nk, cols

            def read_before(l, n, j, s):
                if s % 3 < 2:
                    w_loop(sp, a_p, a_p.at(l, 2 * (n - 2) + 1 + s % 3) + 4 * j)
                else:
                    w_loop(sp, y_p, y_p.at(l, 2 * (n - 2) + 2) + 4 * j)

            held = [None] * 6
            for key in plan:
                if key[0] != "experts":
                    s = slot_of[key]
                    if held[s] is not None:
                        sp.wait_ge(*last_read(held[s]))
                    if key[0] == "mod" and key[2] == MOD_A and key[1] > 0:
                        sp.wait_ge(bias_in, 16 * (2 * key[1] + 1))
                    if key[1] in guest:
                        sp.wait_ge(*last_read((key[0], guest[key[1]])))
                    load(s, *source(key))
                    held[s] = key
                    continue
                l = key[1]
                tiles = [tile for half in range(2) for tile in expert(l, half, half)]
                for n in ((4, 5, 0, 1, 3, 2) if l + 1 < LAYERS else (0, 2, 3, 1, 4, 5)):
                    s, src, nk, cols = tiles[n]
                    if s < 4:
                        sp.wait_ge(*last_read(held[s]))
                    elif s == 4:
                        w(sp, h2_p, l, NT)
                        w(sp, h2_out, l, 16 * NT)
                    load(s, src, nk, cols)
                with sp.Fori(1, PAIRS) as j:
                    for half in range(2):
                        for s, src, nk, cols in expert(l, 2 * j + half, half):
                            read_before(l, half, j, s)
                            load(s, src, nk, cols)
                w(sp, y_p, l, 4 * PAIRS)
                n_over = sp.value_load(slots_u[0:1, N_OVER:N_OVER + 1], min_val=0, max_val=9)
                with sp.If(n_over > 0):
                    with sp.Fori(0, OVER_PAIRS) as j:
                        for half in range(2):
                            e = sp.value_load(slots_u[0:1, bass.ds(2 * j + (E_OVER + half), 1)],
                                              min_val=0, max_val=NE - 1)
                            for s, src, nk, cols in expert(l, e, half):
                                read_before(l, NE + half, j, s)
                                load(s, src, nk, cols)
                with sp.Else():
                    for s in range(6):
                        sp.sem_inc(full[s], 16 * OVER_PAIRS)
                w(sp, y_p, l, 2 * NB2)
                held = [None] * 6

        xn = w_(6144, NT * D).rearrange("p (t d) -> p t d", t=NT)
        sq1 = w_(5120, D)
        zr = w_(0, NT * 3 * 512).rearrange("p (t i c) -> p t i c", t=NT, i=3)
        qT = w_(7680, 4 * T).rearrange("p (i t) -> p i t", i=4)
        kT = w_(10240, 768)
        zq = w_(11264, NT * 768).rearrange("p (t c) -> p t c", t=NT)
        prob = [w_(15104 + 640 * b, 640) for b in range(2)]
        dec_tmp = w_(15104, 1024).rearrange("p (f h i) -> p f h i", f=2, h=HR)
        rope_tmp = w_(15104, 1024)
        probT = [w_(16384 + 640 * b, 640) for b in range(2)]
        qk_tmp = w_(16384, 640)
        st_tmp = w_(7680, 512)
        st_buf = [w_(7680, 512), w_(8192, 512)]
        kdec = [w_(8704, 512), w_(9216, 512)]
        o_tmp = w_(8704, 512)
        sb_st = [w_(9728 + 512 * n, 512) for n in range(NS)]
        sf_st = [w_(11776 + 512 * n, 512) for n in range(NS)]
        rqT, rqTf, rqTb, rkT = (w_(13824 + 512 * n, 512).rearrange("p (h i) -> p h i", h=HR) for n in range(4))
        inner = [w_(15872 + 512 * b, 512).rearrange("p (h i) -> p h i", h=HR) for b in range(2)]
        sgr = w_(16896, 512)
        gu = w_(8192, NT * 512).rearrange("p (t c) -> p t c", t=NT)
        gv = w_(10752, NT * 512).rearrange("p (t c) -> p t c", t=NT)
        cmb = [w_(13824 + 512 * b, 512) for b in range(2)]
        mlp_tmp = w_(13312, 512)
        mixT = w_(8192, KD * T).rearrange("p (k t) -> p k t", k=KD)
        sg = [w_(13312 + 640 * b, 640) for b in range(2)]
        mix_tmp = w_(14592, 640)
        gate1 = w_(15232, 2 * D).rearrange("p (s d) -> p s d", s=2)
        xh = hT[:, :].rearrange("p (t d) -> p t d", t=NT)
        out_tmp = w_(13312, 512)
        sq2 = w_(13824, D)
        h2 = w_(0, NT * D).rearrange("p (t d) -> p t d", t=NT)
        shift2 = [w_(5120, D), branch[:, 5120:6144]]
        gain2 = [w_(6144, D), branch[:, 6144:7168]]
        norm2_row = w_(7168, D)
        h2T = branch[:, 0:KD * T].rearrange("p (k t) -> p k t", k=KD)
        slot_oh = [w_(8192 + NT * P * n, NT * P).rearrange("p (t s) -> p t s", t=NT) for n in range(2)]
        block_oh = [w_(9472 + NT * NTAB * n, NT * NTAB).rearrange("p (t b) -> p t b", t=NT) for n in range(2)]
        mod_batch = {0: (11264, 0), 1: (13312, 0), 2: (15360, MOD_A)}
        xb = [w_(8192 + D * b, D) for b in range(2)]
        xbT = [w_(10240 + D * b, D) for b in range(2)]
        sa = [w_(12288 + 512 * b, 512) for b in range(2)]
        hd = [w_(13312 + 512 * b, 512) for b in range(2)]
        hdT = [w_(14336 + 512 * b, 512) for b in range(2)]
        yb = [w_(15360 + D * b, D) for b in range(2)]
        y1 = [w_(11264 + 2 * D * b, D) for b in range(2)]
        y2 = [w_(11264 + 2 * D * b + D, D) for b in range(2)]
        gate2 = branch[:, 0:2 * D].rearrange("p (s d) -> p s d", s=2)
        zeros = branch[:, 8 * T:8 * T + 512]
        cond_rows = hT[0:16, 0:P]
        at[0] = 8 * T
        (r_sc, r_sel, r_mask, r_oh0, r_oh1, r_oh, r_tmp, r_masked) = (
            take(branch, NT * NE).rearrange("p (t e) -> p t e", t=NT) for _ in range(8))
        r_m1, r_n1, r_m2, r_n2 = (take(branch, NT * NG) for _ in range(4))
        r_gs = take(branch, NT * 8).rearrange("p (t e) -> p t e", t=NT)
        r_top = take(branch, NT * 8).rearrange("p (t e) -> p t e", t=NT)
        r_gi = take(branch, NT * 8).bitcast(U32).rearrange("p (t e) -> p t e", t=NT)
        r_ei = take(branch, NT * 8).bitcast(U32).rearrange("p (t e) -> p t e", t=NT)
        r_gf = take(branch, NT)
        r_ef = [take(branch, NT) for _ in range(2)]
        r_w = [take(branch, NT) for _ in range(2)]
        r_wn = [take(branch, NT) for _ in range(2)]
        r_rank = [take(branch, NT) for _ in range(2)]
        r_dest = [take(branch, NT) for _ in range(2)]
        r_hi, r_ob, r_sum, r_fl = (take(branch, NT) for _ in range(4))
        r_cnt, r_ov, r_c0, r_c1, r_ex = (take(branch, NE) for _ in range(5))
        r_le = take(branch, OVER * NE).rearrange("p (b e) -> p b e", b=OVER)
        r_eo = take(branch, OVER)
        r_mod = [take(branch, NT) for _ in range(2)]
        assert at[0] <= 12 * T, at[0]

        def flat(a):
            return a.rearrange("p a b -> p (a b)")

        def heads(a):
            return a.rearrange("p (h i) -> p h i", h=HR)

        def bank(b, n=512):
            return ps[:, b, 0:n]

        def two(b):
            return ps[:, b:b + 2, :].rearrange("p b c -> p (b c)")[:, 0:T]

        def halves(b):
            return ps[:, b:b + 2, 0:T // 2]

        def in_halves(a):
            return a.rearrange("p (s c) -> p s c", s=2)

        def cond_of(tt):
            return 1 if tt == PROMPT else 0

        def mod_at(batch, t, part):
            base, first = mod_batch[batch]
            c = base + (t - first) * 512
            return work[part, c:c + 512]

        def tok(tt):
            return slice(tt * P, (tt + 1) * P)

        @block.tensor
        def _(pe):
            def mm(out, lhsT, rhs, k, n):
                return pe.matmul(out, lhsT, rhs, start=(k == 0), stop=(k == n - 1))

            def mod_tile(batch, l, t):
                n = l * MODT + t
                if n >= 2:
                    pe.wait_ge(mod_ev, n - 1)
                s = slot_of["mod", l, t]
                pe.wait_ge(full[s], full_at(("mod", l, t)))
                out = ps[0:2, 4 + t % 2, :]
                for k in range(KD):
                    pe.matmul(out, scT[:, k:16:KD], slot[s][:, k * 512:(k + 1) * 512], start=(k == 0), stop=False)
                pe.matmul(out, ones[64:65, 0:2], mod_at(batch, t, slice(64, 65)), start=False,
                          stop=True).then_inc(mod_mm, 1)

            pe.wait_ge(cond_in, 16 * 3)
            pe.transpose(ps[:, 7, 0:16], cond_rows, ident[0:16, 0:16]).then_inc(cond_t, 1)
            pe.wait_ge(cond_s, 1)
            pe.wait_ge(bias_in, 16)
            for t in range(MODT):
                mod_tile(0, 0, t)

            for l in range(LAYERS):
                def loaded(name):
                    s = slot_of[l, name]
                    pe.wait_ge(full[s], full_at((l, name)))
                    return slot[s]

                if l > 0:
                    w(pe, hd_v, l - 1, NB2)
                    pe.wait_ge(bias_in, 16 * (2 * l + 1))
                    for t in range(MOD_A, MODT):
                        mod_tile(2, l, t)
                    w(pe, y_a, l - 1, 2 * NB2)
                pe.wait_ge(mod_ev, MODT * (l + 1))
                w(pe, aux_in, l, aux_in.per)
                w(pe, modr_in, l, 32)
                pe.transpose(ps[:, 4, 0:40], mod_rows, ident[0:40, 0:40]).then_inc(au_p.sem, 1)
                for g in range(4):
                    i = pe.transpose(ps[:, 5, g * P:(g + 1) * P], ws_raw[:, g * P:(g + 1) * P], ident)
                i.then_inc(au_p.sem, 1)

                def turn_in(tt):
                    w(pe, xn_v, l, tt + 1)
                    if tt >= 2:
                        w(pe, h_a, l, tt - 1)
                        w(pe, h_v, l, tt - 1)
                    for k in range(KD):
                        i = pe.transpose(ps[:, 2 * (tt % 2) + k // 4, (k % 4) * P:(k % 4 + 1) * P],
                                         xn[:, tt, k * P:(k + 1) * P], ident)
                    i.then_inc(tr_p.sem, 1)

                def project(g, name, tt, cols):
                    wt = loaded(name)
                    if g >= 4:
                        w(pe, z_a, l, g - 3)
                    for k in range(KD):
                        i = mm(bank(4 + g % 4, cols), h3[:, k, tok(tt)], wt[:, k * cols:(k + 1) * cols], k, KD)
                    i.then_inc(z_p.sem, 1)

                turn_in(0)
                turn_in(1)
                w(pe, ws_v, l, 1)
                w(pe, mc_v, l, 2)
                for tt in range(NT):
                    w(pe, h_a, l, tt + 1)
                    w(pe, h_v, l, tt + 1)
                    project(2 * tt, "q", tt, 512)
                    project(2 * tt + 1, "kv", tt, 256)
                    if tt + 2 < NT:
                        turn_in(tt + 2)
                def project_split(s, name, tt):
                    g = (2 + s) * NT + tt
                    w(pe, z_a, l, g - 3)
                    w(pe, hs_v, l, tt + 1)
                    w(pe, zl_g, l, s + 1)
                    w_hi_z, w_lo_z = slot_r[high_slot[name]], slot_r[slot_of[l, name]]
                    for k in range(KD):
                        h_hi_k = h_high[k // 4][:, (k % 4) * T + tt * P:(k % 4) * T + (tt + 1) * P]
                        h_lo_k = h_lo[:, k * T + tt * P:k * T + (tt + 1) * P]
                        for m, (hk, wk) in enumerate(((h_hi_k, w_hi_z), (h_hi_k, w_lo_z), (h_lo_k, w_hi_z))):
                            i = mm(bank(4 + g % 4), hk, wk[:, k * 512:(k + 1) * 512], 3 * k + m, 3 * KD)
                    i.then_inc(z_p.sem, 1)

                def turn_qk(tt):
                    if tt >= 2:
                        w(pe, qt_a, l, tt - 1)
                    if tt < NT:
                        w(pe, qk_v, l, tt + 1)
                        for i4 in range(4):
                            pe.transpose(ps[:, tt % 2, i4 * P:(i4 + 1) * P], zq[:, tt, i4 * P:(i4 + 1) * P], ident)
                    src = zq[:, tt, 512:640] if tt < NT else kc_raw
                    pe.transpose(ps[:, 2 + tt % 2, 0:P], src, ident).then_inc(qt_p.sem, 1)

                for s, name in enumerate(("qr", "kr")):
                    for tt in range(NT):
                        project_split(s, name, tt)
                for tt in range(NT - 1):
                    for t2 in QK_TURNS[tt]:
                        turn_qk(t2)
                    project_split(2, "vr", tt)


                def score(u):
                    tt, h = divmod(u, HQ)
                    half, i4 = divmod(h, 4)
                    b = 2 * (u % 2)
                    if u >= 2:
                        w(pe, e_a, l, u - 1)
                    part = slice(half * DH, half * DH + DH)
                    if tt < NS:
                        pe.matmul(bank(b), qT[part, i4, tok(tt)], kT[part, 0:512], start=True, stop=True)
                        i = pe.matmul(bank(b + 1, P), qT[part, i4, tok(tt)], kT[part, 512:640], start=True, stop=True)
                    else:
                        i = pe.matmul(bank(b, P), qT[part, i4, tok(tt)], kT[part, 640:768], start=True, stop=True)
                    i.then_inc(s_p.sem, 1)

                def turn_probs(u):
                    w(pe, e_a, l, u + 1)
                    if u >= 1:
                        w(pe, pt_a, l, u)
                    nk = 5 if u // HQ < NS else 1
                    for c in range(nk):
                        out = ps[:, 4, c * P:(c + 1) * P] if c < 4 else ps[:, 5, 0:P]
                        i = pe.transpose(out, prob[u % 2][:, c * P:(c + 1) * P], ident)
                    i.then_inc(pt_p.sem, 1)

                def values(u):
                    tt, h = divmod(u, HQ)
                    kv = 640 + DH * (h // 4)
                    w(pe, pt_a, l, u + 1)
                    if h == 0 and tt >= 2:
                        w(pe, at_a, l, tt - 1)
                    nk = 5 if tt < NS else 1
                    for c in range(nk):
                        if tt == PROMPT:
                            v = zq[:, PROMPT, kv:kv + DH]
                        elif c < NS:
                            v = zq[:, c, kv:kv + DH]
                        else:
                            v = v_cache[:, kv - 640:kv - 640 + DH]
                        i = mm(ps[:, 6 + tt % 2, h * DH:(h + 1) * DH], probT[u % 2][:, c * P:(c + 1) * P], v, c, nk)
                    i.then_inc(pv_p.sem, 1)

                def turn_att(tt):
                    w(pe, at_v, l, tt + 1)
                    for c in range(4):
                        i = pe.transpose(ps[:, 6 + tt % 2, c * P:(c + 1) * P], zq[:, tt, c * P:(c + 1) * P], ident)
                    i.then_inc(at_p.sem, 1)

                NU = NT * HQ
                w(pe, qt_a, l, NT + 1)
                score(0)
                project_split(2, "vr", NT - 1)
                for u in range(NU):
                    if u + 1 < NU:
                        score(u + 1)
                    if u == 0:
                        w(pe, z_a, l, 5 * NT)
                    turn_probs(u)
                    if u >= 1:
                        values(u - 1)
                    if u >= 11 and (u - 11) % HQ == 0:
                        turn_att((u - 11) // HQ)
                values(NU - 1)
                turn_att(NT - 1)

                w(pe, e_a, l, NU)
                for n, (_, tt) in enumerate(STATES):
                    w(pe, kd_g, l, n + 1)
                    if n >= 2:
                        w(pe, kv_v, l, n - 1)
                    for h in range(HR):
                        hs = slice(h * P, (h + 1) * P)
                        i = pe.matmul(ps[:, n % 2, hs], kdec[n % 2][:, hs], zr[:, tt, 2, hs], start=True, stop=True)
                    i.then_inc(kv_p.sem, 1)

                def turn_ret(tt):
                    w(pe, rn_v, l, tt + 1)
                    if tt >= 1:
                        w(pe, rt_ev, l, tt)
                    for c in range(4):
                        i = pe.transpose(ps[:, 7, c * P:(c + 1) * P], o_tmp[:, c * P:(c + 1) * P], ident)
                    i.then_inc(rt_p.sem, 1)

                w(pe, pt_a, l, NU)
                w(pe, at_a, l, NT)
                wt = loaded("gr")
                w(pe, hr_g, l, 2)
                w(pe, kv_v, l, 2 * (NS - 1))
                w(pe, st_a, l, 2)
                for tt in range(NT):
                    for src, b, sig_p, sig_e in ((0, 2, rq_p, rq_v), (1, 3, rk_p, rk_a)):
                        if tt >= 1:
                            w(pe, sig_e, l, tt)
                        for h in range(HR):
                            i = pe.transpose(ps[:, b, h * P:(h + 1) * P], zr[:, tt, src, h * P:(h + 1) * P], ident)
                        i.then_inc(sig_p.sem, 1)
                    if tt >= 1:
                        w(pe, gr_a, l, tt)
                    for k in range(KD):
                        i = mm(bank(5), h3[:, k, tok(tt)], wt[:, k * 512:(k + 1) * 512], k, KD)
                    i.then_inc(gr_p.sem, 1)
                    w(pe, rq_v, l, tt + 1)
                    w(pe, rk_a, l, tt + 1)
                    if tt >= 1:
                        w(pe, in_v, l, tt)
                    for h in range(HR):
                        i = pe.matmul(ps[:, 4, h * P:(h + 1) * P], rkT[:, h, :], rqT[:, h, :], start=True, stop=True)
                    i.then_inc(in_p.sem, 1)
                    if tt >= 1:
                        turn_ret(tt - 1)
                    w(pe, in_v, l, tt + 1)
                    for h in range(HR):
                        hs = slice(h * P, (h + 1) * P)
                        n = 3 if tt < NS else 1
                        i = mm(ps[:, 6, hs], inner[tt % 2][:, h, :], zr[:, tt, 2, hs], 0, n)
                        if tt < NS:
                            mm(ps[:, 6, hs], rqTf[:, h, :], sf_st[tt][:, hs], 1, n)
                            i = mm(ps[:, 6, hs], rqTb[:, h, :], sb_st[tt][:, hs], 2, n)
                    i.then_inc(o_p.sem, 1)

                w(pe, kv_v, l, 8)
                w(pe, rq_v, l, NT)
                w(pe, rk_a, l, NT)
                for s, name in enumerate(("mu", "mv")):
                    wt = loaded(name)
                    for tt in range(NT):
                        g = s * NT + tt
                        if g >= 4:
                            w(pe, m_a, l, g - 3)
                        for k in range(KD):
                            i = mm(bank(g % 4), h3[:, k, tok(tt)], wt[:, k * 512:(k + 1) * 512], k, KD)
                        i.then_inc(m_p.sem, 1)
                        if g == 0:
                            turn_ret(NT - 1)
                w(pe, in_v, l, NT)
                w(pe, gr_a, l, NT)
                w(pe, rt_ev, l, NT)

                def turn_cm(tt):
                    w(pe, cm_v, l, tt + 1)
                    if tt >= 2:
                        w(pe, cm_a, l, tt - 1)
                    for c in range(4):
                        i = pe.transpose(ps[:, 6 + tt % 2, c * P:(c + 1) * P], cmb[tt % 2][:, c * P:(c + 1) * P], ident)
                    i.then_inc(cm_p.sem, 1)

                for tt in range(NT):
                    w(pe, vn_v, l, tt + 1)
                    if tt >= 2:
                        w(pe, cm_v, l, tt - 1)
                    for g in range(4):
                        gs = slice(g * P, (g + 1) * P)
                        i = pe.matmul(ps[:, 4 + tt % 2, gs], wsT[:, gs], gv[:, tt, gs], start=True, stop=True)
                    i.then_inc(f_p.sem, 1)
                    if tt >= 1:
                        turn_cm(tt - 1)
                turn_cm(NT - 1)

                w(pe, m_a, l, 2 * NT)
                w(pe, cm_v, l, NT)
                w(pe, cm_a, l, NT)
                w(pe, hh_v, l, 1)
                w(pe, hl_g, l, 2)
                hi3 = h_hi.rearrange("p (k t) -> p k t", k=KD)
                lo3 = h_lo.rearrange("p (k t) -> p k t", k=KD)
                for br, src in enumerate((attT, retT, cmT)):
                    wo = None
                    for c in range(KD):
                        n = 8 * br + c
                        if c == 0:
                            wo = loaded(f"o{br}")
                        b = 2 * (n % 2)
                        if n >= 2:
                            w(pe, g_a, l, n - 1)
                        gc = (c % 4) * P
                        w(pe, wg_v, l, n + 1)
                        w_lo = slot_r[slot_of[l, f"g{br}{c // 4}"]]
                        for k in range(KD):
                            wg = w_hi[n % 3][:, k * P:(k + 1) * P]
                            products = ((wg, hi3), (wg, lo3), (w_lo[:, k * 512 + gc:k * 512 + gc + P], hi3))
                            for m, (wk, hk) in enumerate(products):
                                for half in range(2):
                                    i = mm(bank(b + half, T // 2), wk, hk[:, k, half * T // 2:(half + 1) * T // 2],
                                           3 * k + m, 3 * KD)
                        i.then_inc(g_p.sem, 1)
                        if n >= 2:
                            w(pe, mix_v, l, n - 1)
                        for half in range(2):
                            for k in range(4):
                                i = mm(bank(4 + b + half, T // 2), wo[:, k * D + c * P:k * D + (c + 1) * P],
                                       src[:, k, half * T // 2:(half + 1) * T // 2], k, 4)
                        i.then_inc(o3_p.sem, 1)
                w(pe, mix_v, l, 24)

                def turn_h2(tt):
                    w(pe, h2_v, l, tt + 1)
                    if tt >= 2:
                        w(pe, h2_a, l, tt - 1)
                        w(pe, h2_q, l, tt - 1)
                    for k in range(KD):
                        i = pe.transpose(ps[:, 4 + 2 * (tt % 2) + k // 4, (k % 4) * P:(k % 4 + 1) * P],
                                         h2[:, tt, k * P:(k + 1) * P], ident)
                    i.then_inc(h2_p.sem, 1)

                for tt in range(NT):
                    for half in range(2):
                        q = 2 * tt + half
                        wt = loaded(f"out{half}")
                        if q >= 4:
                            w(pe, x_v, l, q - 3)
                        for k in range(KD):
                            i = mm(bank(q % 4), mixT[:, k, tok(tt)], wt[:, k * 512:(k + 1) * 512], k, KD)
                        i.then_inc(w_p.sem, 1)
                    if tt >= 1:
                        turn_h2(tt - 1)
                turn_h2(NT - 1)
                pe.wait_ge(const_in, 32)
                w(pe, h2_a, l, NT)
                w(pe, h2_q, l, NT)
                for tt in range(NT):
                    for k in range(KD):
                        i = mm(ps[:, 0, tt * NE:(tt + 1) * NE], h2T[:, k, tok(tt)], w_rt[:, k * NE:(k + 1) * NE], k, KD)
                i.then_inc(lo_p.sem, 1)

                def next_mods(first, last):
                    if l + 1 < LAYERS:
                        for t in range(first, last):
                            mod_tile(1, l + 1, t)

                if l + 1 < LAYERS:
                    pe.wait_ge(bias_in, 16 * (2 * l + 2))
                next_mods(0, 3)
                w(pe, oh_v, l, 1)
                for tt in range(NT):
                    out = ps[:, 1, tt * NE:(tt + 1) * NE]
                    for t2 in range(tt):
                        mm(out, ones, r_oh[:, t2, :], t2, tt + 1)
                    mm(out, before, r_oh[:, tt, :], tt, tt + 1)
                for tt in range(NT):
                    i = mm(ps[:, 1, 80:96], ones, r_oh[:, tt, :], tt, NT)
                i.then_inc(rk_p2.sem, 1)
                next_mods(3, 6)
                for n in range(2):
                    w(pe, tab_v, l, n + 1)
                    for tt in range(NT):
                        i = mm(ps[:, 2, 0:NTAB], slot_oh[n][:, tt, :], block_oh[n][:, tt, :], n * NT + tt, 2 * NT)
                i.then_inc(tk_p.sem, 1)
                next_mods(6, MOD_A)
                w(pe, tk_v, l, 1)

                def turn_x(b, n, j=None):
                    on = 0 if j is None else 1
                    pe.wait_ge(xb_in[b].sem, xb_in[b].at(l, 16 * ((n - b) // 2 + 1)) + (16 * j if on else 0))
                    if n >= 1:
                        pe.wait_ge(xt_a.sem, xt_a.at(l, n) + (2 * j if on else 0))
                    for c in range(KD):
                        i = pe.transpose(ps[:, c // 4, (c % 4) * P:(c % 4 + 1) * P],
                                         xb[b][:, c * P:(c + 1) * P], ident)
                    i.then_inc(xt_p.sem, 1)

                def pair(j, n0, u0):
                    def got(s):
                        pe.wait_ge(full[s], 16 * j + 16 * (expert_base[l][s] + u0 + 1))
                        return slot[s]

                    def gate(b):
                        pe.wait_ge(xt_a.sem, xt_a.at(l, n0 + b + 1) + 2 * j)
                        pe.wait_ge(y_a.sem, y_a.at(l, 2 * (n0 + b) - 2) + 4 * j)
                        wt = got(3 * b)
                        for k in range(KD):
                            i = mm(bank(2 + b), xbT[b][:, k * P:(k + 1) * P], wt[:, k * 512:(k + 1) * 512], k, KD)
                        i.then_inc(a_p.sem, 1)

                    def up(b):
                        wt = got(3 * b + 1)
                        for k in range(KD):
                            i = mm(bank(4 + b), xbT[b][:, k * P:(k + 1) * P], wt[:, k * 512:(k + 1) * 512], k, KD)
                        i.then_inc(a_p.sem, 1)

                    def turn_h(b):
                        pe.wait_ge(hd_v.sem, hd_v.at(l, n0 + b + 1) + 2 * j)
                        for c in range(4):
                            i = pe.transpose(ps[:, 6, c * P:(c + 1) * P], hd[b][:, c * P:(c + 1) * P], ident)
                        i.then_inc(ht_p.sem, 1)

                    def down(b):
                        pe.wait_ge(ht_v.sem, ht_v.at(l, n0 + b + 1) + 2 * j)
                        wt = got(3 * b + 2)
                        for half in range(2):
                            if half == 0:
                                pe.wait_ge(y_a.sem, y_a.at(l, 2 * (n0 + b) - 1) + 4 * j)
                            for k in range(4):
                                i = mm(bank(2 + b if half else 7), hdT[b][:, k * P:(k + 1) * P],
                                       wt[:, k * D + half * 512:k * D + half * 512 + 512], k, 4)
                            i.then_inc(y_p.sem, 1)

                    gate(0)
                    up(0)
                    turn_x(1, n0 + 1, j)
                    gate(1)
                    turn_h(0)
                    up(1)
                    down(0)
                    turn_h(1)
                    turn_x(0, n0 + 2, j)
                    down(1)

                turn_x(0, 0)
                with pe.Fori(0, PAIRS) as j:
                    pair(j, 0, 0)
                n_over = pe.value_load(slots_u[0:1, N_OVER:N_OVER + 1], min_val=0, max_val=9)
                w(pe, y_p, l, 4 * PAIRS)
                with pe.If(n_over > 0):
                    with pe.Fori(0, OVER_PAIRS) as j:
                        pair(j, NE, PAIRS)
                with pe.Else():
                    pe.sem_inc(xt_p.sem, OVER)
                    pe.sem_inc(a_p.sem, 2 * OVER)
                    pe.sem_inc(ht_p.sem, OVER)
                    pe.sem_inc(y_p.sem, 2 * OVER)
        @block.scalar
        def _(act):
            A = act.activation
            for n, nm in enumerate(("c", "c_ctx")):
                src = I[nm].rearrange("o (k p) -> (o k) p", p=P) if nm == "c" else I[nm].rearrange("(k p) -> k p", p=P)
                act.dma_start(cond_rows[KD * n:KD * n + KD, :], src).then_inc(cond_in, 16)
            act.dma_start(const[:, :], I["persistent"]).then_inc(cond_in, 16)
            act.sem_inc(y_a.sem, y_a.before)
            for b in range(2):
                act.sem_inc(y_out[b].sem, y_out[b].before)
            act.wait_ge(cond_t, 1)
            A(scT, ps[:, 7, 0:16], ACT.Silu).then_inc(cond_s, 1)
            step = Steps(act, a_step)
            roots = [0]

            def root(l, ap):
                roots[0] += 1
                act.wait_ge(ms_v.sem, roots[0])
                A(ap, ap, ACT.Sqrt).then_inc(rt_a.sem, 1)

            def take_mod(batch, l, t):
                act.wait_ge(mod_mm, l * MODT + t + 1)
                A(mod_at(batch, t, slice(0, 2)), ps[0:2, 4 + t % 2, :], ACT.Copy).then_inc(mod_ev, 1)

            def square_in(tt):
                A(sq1, xr[:, tt, :], ACT.Square, accum_out=st[:, tt:tt + 1]).then_inc(ssq1.sem, 1)

            act.wait_ge(xin, 32)
            for tt in range(NT):
                take_mod(0, 0, tt)
                if tt >= 1:
                    act.wait_ge(ssq1.sem, tt)
                square_in(tt)
                root(0, st[:, tt:tt + 1])
            for t in range(NT, MODT):
                take_mod(0, 0, t)

            for l in range(LAYERS):
                def modulate(tt):
                    w(act, tr_p, l, tt + 1)
                    c0 = 16 * cond_of(tt)
                    for k in range(4):
                        i = A(h3[:, k, tok(tt)], ps[:, 2 * (tt % 2), k * P:(k + 1) * P], ACT.Identity,
                              bias=modc[:, c0 + k:c0 + k + 1], scale=modc[:, c0 + KD + k:c0 + KD + k + 1])
                    i.then_inc(h_a.sem, 1)

                def take_z(g):
                    if g < 2 * NT:
                        tt, s = divmod(g, 2)
                        dst, n = (zq[:, tt, 0:512], 512) if s == 0 else (zq[:, tt, 512:768], 256)
                    else:
                        s, tt = divmod(g, NT)
                        dst, n = zr[:, tt, s - 2, :], 512
                    w(act, z_p, l, g + 1)
                    if g == 2 * NT:
                        w(act, xs_out, l, 16)
                    retention_k = g >= 2 * NT and s == 3
                    A(dst, bank(4 + g % 4, n), ACT.Copy, scale=(float(P) ** -0.5 if retention_k else 1.0)
                      ).then_inc(z_a.sem, 1)

                w(act, mc_v, l, 2)
                if l > 0:
                    w(act, cb_v, l - 1, NT)
                act.wait_ge(mod_st, 32 * (l + 1))
                modulate(0)
                modulate(1)
                for tt in range(NT):
                    take_z(2 * tt)
                    take_z(2 * tt + 1)
                    if tt + 2 < NT:
                        modulate(tt + 2)
                w(act, aux_in, l, aux_in.per)
                step.do(A(lg, lg, ACT.Exp))
                step.do(A(lg, lg, ACT.Copy, scale=-1.0))
                for f in range(2):
                    for h in range(HR):
                        s_ = lg[:, 4 * f + h:4 * f + h + 1]
                        A(dec_q[:, f, h, :], dist[:, (4 + f) * P:(5 + f) * P], ACT.Exp, scale=s_)
                        A(dec_tmp[:, f, h, :], dist[:, 2 * f * P:(2 * f + 1) * P], ACT.Exp, scale=s_)
                    A(dec_k[:, 4 * f:4 * f + 4], lg[:, 4 * f:4 * f + 4], ACT.Exp, scale=kpos[:, f:f + 1])
                A(dec_chunk, lg, ACT.Exp, scale=float(P)).then_inc(dec_a.sem, 1)
                for g in range(2 * NT, 4 * NT):
                    take_z(g)
                    if g == 2 * NT + 1:
                        root(l, st[:, 0:50])
                def take_qk(tt):
                    w(act, qt_p, l, tt + 1)
                    if tt < NT:
                        A(qT[:, :, tok(tt)], heads(bank(tt % 2)), ACT.Copy, scale=float(DH) ** -0.5)
                    k0 = tt * P if tt < NS else (640 if tt == PROMPT else 512)
                    A(kT[:, k0:k0 + P], bank(2 + tt % 2, P), ACT.Copy).then_inc(qt_a.sem, 1)

                for tt in range(NT - 1):
                    for t2 in QK_TURNS[tt]:
                        take_qk(t2)
                    take_z(4 * NT + tt)

                def exp_unit(u):
                    n = 640 if u // HQ < NS else P
                    w(act, mx_v, l, u + 1)
                    A(prob[u % 2][:, 0:n], two(2 * (u % 2))[:, 0:n], ACT.Exp, bias=negmax[:, u:u + 1],
                      accum_out=psums[:, u:u + 1]).then_inc(e_a.sem, 1)

                def take_att(tt):
                    w(act, at_p, l, tt + 1)
                    w(act, hr_g, l, 2)
                    A(attT[:, :, tok(tt)], heads(bank(6 + tt % 2)), ACT.Copy).then_inc(at_a.sem, 1)

                NU = NT * HQ
                exp_unit(0)
                take_z(5 * NT - 1)
                for u in range(NU):
                    if u + 1 < NU:
                        exp_unit(u + 1)
                    w(act, pt_p, l, u + 1)
                    n = 640 if u // HQ < NS else P
                    A(probT[u % 2][:, 0:n], two(4)[:, 0:n], ACT.Copy).then_inc(pt_a.sem, 1)
                    if u >= 12 and (u - 12) % HQ == 0:
                        take_att((u - 12) // HQ)
                take_att(NT - 1)
                A(sf_st[0], s_raw[:, 0:512], ACT.Copy).then_inc(st_a.sem, 1)
                A(sb_st[NS - 1], s_raw[:, 512:1024], ACT.Copy).then_inc(st_a.sem, 1)
                def take_ret(tt):
                    w(act, rt_p, l, tt + 1)
                    A(retT[:, :, tok(tt)], heads(bank(7)), ACT.Copy).then_inc(rt_ev.sem, 1)

                for tt in range(NT):
                    w(act, rk_p, l, tt + 1)
                    if tt >= 1:
                        w(act, in_p, l, tt)
                    A(flat(rkT), bank(3), ACT.Copy).then_inc(rk_a.sem, 1)
                    w(act, gr_p, l, tt + 1)
                    if tt >= 1:
                        w(act, rn_v, l, tt)
                    A(sgr, bank(5), ACT.Silu).then_inc(gr_a.sem, 1)
                    if tt >= 1:
                        take_ret(tt - 1)
                    root(l, bna[:, 0:4])
                take_ret(NT - 1)
                w(act, st_out, l, 32)
                for g in range(2 * NT):
                    w(act, m_p, l, g + 1)
                    A((gu if g < NT else gv)[:, g % NT, :], bank(g % 4), ACT.Gelu_apprx_tanh).then_inc(m_a.sem, 1)
                root(l, st[:, 0:NT])
                act.wait_ge(y_zero, 32)
                for tt in range(NT):
                    w(act, cm_p, l, tt + 1)
                    A(cmT[:, :, tok(tt)], heads(bank(6 + tt % 2)), ACT.Copy).then_inc(cm_a.sem, 1)
                for n in range(24):
                    w(act, g_p, l, n + 1)
                    if n >= 2:
                        w(act, mix_v, l, n - 1)
                    A(in_halves(sg[n % 2]), halves(2 * (n % 2)), ACT.Sigmoid).then_inc(g_a.sem, 1)
                def take_h2(tt):
                    w(act, h2_p, l, tt + 1)
                    A(h2T[:, 0:4, tok(tt)], heads(bank(4 + 2 * (tt % 2))), ACT.Copy).then_inc(h2_a.sem, 1)

                for tt in range(NT):
                    w(act, x_v, l, 2 * tt + 2)
                    if tt >= 1:
                        w(act, ssq2, l, tt)
                    A(sq2, xh[:, tt, :], ACT.Square, accum_out=st[:, tt:tt + 1]).then_inc(ssq2.sem, 1)
                    root(l, st[:, tt:tt + 1])
                    if tt >= 1:
                        take_h2(tt - 1)
                take_h2(NT - 1)
                w(act, lo_p, l, 1)
                A(flat(r_sc), bank(0, NT * NE), ACT.Sigmoid).then_inc(sc_a.sem, 1)
                if l + 1 < LAYERS:
                    for t in range(MOD_A):
                        take_mod(1, l + 1, t)
                w(act, tk_v, l, 1)

                def pair(j, n0):
                    def take_x(b, n):
                        act.wait_ge(xt_p.sem, xt_p.at(l, n + 1) + 2 * j)
                        A(xbT[b], ps[:, 0:2, :].rearrange("p b c -> p (b c)"), ACT.Copy).then_inc(xt_a.sem, 1)

                    def gate(b):
                        act.wait_ge(a_p.sem, a_p.at(l, 2 * (n0 + b) + 1) + 4 * j)
                        A(sa[b], bank(2 + b), ACT.Silu).then_inc(si_a.sem, 1)

                    def store(b):
                        act.wait_ge(y_out[b].sem, y_out[b].at(l, 16 * (n0 // 2)) + 16 * j)
                        for half in range(2):
                            act.wait_ge(y_p.sem, y_p.at(l, 2 * (n0 + b) + half + 1) + 4 * j)
                            A(yb[b][:, half * 512:half * 512 + 512], bank(2 + b if half else 7),
                              ACT.Copy).then_inc(y_a.sem, 1)
                        act.wait_ge(y_a.sem, y_a.at(l, 2 * (n0 + b) + 2) + 4 * j)
                        act.dma_start(y_dram[bass.ds((2 * j + (n0 + b)) * P, P), :], yb[b]).then_inc(y_out[b].sem, 16)

                    gate(0)
                    take_x(1, n0 + 1)
                    gate(1)
                    store(0)
                    take_x(0, n0 + 2)
                    store(1)

                w(act, xt_p, l, 1)
                A(xbT[0], ps[:, 0:2, :].rearrange("p b c -> p (b c)"), ACT.Copy).then_inc(xt_a.sem, 1)
                if l + 1 < LAYERS:
                    act.wait_ge(mod_st, 16 * (2 * l + 3))
                with act.Fori(0, PAIRS) as j:
                    pair(j, 0)
                n_over = act.value_load(slots_u[0:1, N_OVER:N_OVER + 1], min_val=0, max_val=9)
                for b in range(2):
                    w(act, y_out[b], l, 16 * PAIRS)
                with act.If(n_over > 0):
                    with act.Fori(0, OVER_PAIRS) as j:
                        pair(j, NE)
                with act.Else():
                    act.sem_inc(xt_a.sem, OVER)
                    act.sem_inc(si_a.sem, OVER)
                    act.sem_inc(y_a.sem, 2 * OVER)
                    for b in range(2):
                        act.sem_inc(y_out[b].sem, 16 * OVER_PAIRS)
                for b in range(2):
                    w(act, y_out[b], l, 16 * NB2 // 2)

                def weigh(tt):
                    w(act, y1_in[tt % 2], l, 16 * (tt // 2 + 1))
                    A(y1[tt % 2], y1[tt % 2], ACT.Copy, scale=r_wn[0][:, tt:tt + 1]).then_inc(w0_a.sem, 1)

                weigh(0)
                for tt in range(NT):
                    if tt + 1 < NT:
                        weigh(tt + 1)
                    if l + 1 < LAYERS:
                        if tt < MODT - MOD_A:
                            take_mod(2, l + 1, MOD_A + tt)
                        w(act, cb_v, l, tt + 1)
                        if tt >= 1:
                            w(act, ssq1, l + 1, tt)
                        square_in(tt)
                        root(l + 1, st[:, tt:tt + 1])

        @block.vector
        def _(dve):
            V = dve
            TT, TS, STT = V.tensor_tensor, V.tensor_scalar, V.scalar_tensor_tensor
            step = Steps(V, v_step)
            roots = [0]

            def inverse_root(ap, out, inv_n):
                roots[0] += 1
                TS(out=ap, in0=ap, scalar1=inv_n, scalar2=EPS, op0=ALU.mult, op1=ALU.add).then_inc(ms_v.sem, 1)
                V.wait_ge(rt_a.sem, roots[0])
                step.do(V.reciprocal(out, ap))

            def norm_in(l, tt):
                w(V, ssq1, l, tt + 1)
                inverse_root(st[:, tt:tt + 1], st2[:, tt:tt + 1], 1.0 / D)
                TS(out=xn[:, tt, :], in0=xr[:, tt, :], scalar1=st2[:, tt:tt + 1], scalar2=None,
                   op0=ALU.mult).then_inc(xn_v.sem, 1)

            V.wait_ge(xin, 32)
            for tt in range(NT):
                norm_in(0, tt)

            for l in range(LAYERS):
                w(V, au_p, l, 1)
                V.tensor_copy(modc, bank(4, 40)).then_inc(mc_v.sem, 1)
                w(V, au_p, l, 2)
                V.tensor_copy(wsT, bank(5)).then_inc(ws_v.sem, 1)
                w(V, mc_v, l, 1)
                gains = modc[:, 0:32].rearrange("p (s m k) -> p s m k", s=2, m=2)[:, :, 1, :]
                STT(out=gains, in0=gains, scalar=1.0, in1=modc[:, 32:40].unsqueeze(1).broadcast_to([P, 2, KD]),
                    op0=ALU.add, op1=ALU.mult).then_inc(mc_v.sem, 1)
                w(V, mc_v, l, 2)
                def modulate(tt):
                    w(V, tr_p, l, tt + 1)
                    c0 = 16 * cond_of(tt)
                    for k in range(4, KD):
                        i = TS(out=h3[:, k, tok(tt)], in0=ps[:, 2 * (tt % 2) + 1, (k - 4) * P:(k - 3) * P],
                               scalar1=modc[:, c0 + KD + k:c0 + KD + k + 1], scalar2=modc[:, c0 + k:c0 + k + 1],
                               op0=ALU.mult, op1=ALU.add)
                    i.then_inc(h_v.sem, 1)

                def split_h(tt):
                    w(V, z_p, l, 2 * tt + 2)
                    tile = [m.rearrange("p (k t) -> p k t", k=4)[:, :, tok(tt)] for m in h_high]
                    for n in range(2):
                        step.mark(V.tensor_copy(tile[n], h3[:, 4 * n:4 * n + 4, tok(tt)]))
                    step.settle()
                    for n in range(2):
                        i = TT(out=h_lo.rearrange("p (k t) -> p k t", k=KD)[:, 4 * n:4 * n + 4, tok(tt)],
                               in0=h3[:, 4 * n:4 * n + 4, tok(tt)], in1=tile[n].bitcast(F32), op=ALU.subtract)
                    i.then_inc(hs_v.sem, 1)

                def split_z(name):
                    s_ = slot_of[l, name]
                    V.wait_ge(full[s_], full_at((l, name)))
                    if name == "qr":
                        V.wait_ge(mod_mm, MODT * (l + 1))
                    else:
                        w(V, z_p, l, 2 * NT if name == "kr" else 3 * NT)
                    high = slot_r[high_slot[name]]
                    V.tensor_copy(high, slot[s_]).then_inc(zh_v.sem, 1)

                modulate(0)
                modulate(1)
                split_z("qr")
                for tt in range(NT):
                    if tt + 2 < NT:
                        modulate(tt + 2)
                    split_h(tt)
                for tt in range(NT):
                    w(V, z_a, l, 2 * tt + 2)
                    step.do(TT(out=qk_tmp, in0=zq[:, tt, 0:640], in1=zq[:, tt, 0:640], op=ALU.mult))
                    step.do(V.tensor_reduce(st[:, tt * 10:tt * 10 + 10], qk_tmp.rearrange("p (h d) -> p h d", d=DH),
                                            AX.X, ALU.add))
                split_z("kr")
                inverse_root(st[:, 0:50], st2[:, 0:50], 1.0 / DH)
                for tt in range(NT):
                    if tt == 3:
                        split_z("vr")
                    t10 = qk_tmp.rearrange("p (h d) -> p h d", d=DH)
                    z10 = zq[:, tt, 0:640].rearrange("p (h d) -> p h d", d=DH)
                    step.do(TT(out=t10, in0=z10, in1=st2[:, tt * 10:tt * 10 + 10].unsqueeze(2).broadcast_to([P, 10, DH]),
                               op=ALU.mult))
                    for half in range(2):
                        zz = zq[:, tt, 0:512].rearrange("p (i a d) -> p i a d", i=4, a=2)[:, :, half, :]
                        step.mark(TT(out=zz, in0=t10[:, 4 * half:4 * half + 4, :],
                                     in1=qk_gain[:, 0:DH].unsqueeze(1).broadcast_to([P, 4, DH]), op=ALU.mult))
                    i = TT(out=z10[:, 8:10, :], in0=t10[:, 8:10, :],
                           in1=qk_gain[:, DH:2 * DH].unsqueeze(1).broadcast_to([P, 2, DH]), op=ALU.mult)
                    if tt == PROMPT:
                        i.then_inc(qk_v.sem, 1)
                        continue
                    step.do(i)

                    def quarter(ap, b, n):
                        return ap.rearrange("p (h a b n) -> p h a b n", a=2, b=2, n=n)[:, :, :, b, :]

                    def rope(src, tmp, table, dim):
                        nh = src.shape[1] // dim
                        for b in range(2):
                            sin = quarter(table[:, tt, 1, :], b, dim // 4).broadcast_to([P, nh, 2, dim // 4])
                            step.mark(TT(out=quarter(tmp, b, dim // 4), in0=quarter(src, 1 - b, dim // 4), in1=sin,
                                         op=ALU.mult))
                        step.settle()
                        hh = src.rearrange("p (h d) -> p h d", d=dim)
                        step.do(TT(out=hh, in0=hh, in1=table[:, tt, 0, :].unsqueeze(1).broadcast_to([P, nh, dim]),
                                   op=ALU.mult))
                        return TT(out=src, in0=src, in1=tmp, op=ALU.add)

                    rope(zq[:, tt, 0:640], qk_tmp, rope_a, DH).then_inc(qk_v.sem, 1)
                    w(V, qk_v, l, tt + 1)
                w(V, dec_a, l, 1)
                w(V, aux_in, l, aux_in.per)
                for f in range(2):
                    mask = dist[:, (2 * f + 1) * P:(2 * f + 2) * P].unsqueeze(1).broadcast_to([P, HR, P])
                    step.mark(TT(out=dec_tmp[:, f], in0=dec_tmp[:, f], in1=mask, op=ALU.mult))
                step.settle()
                TT(out=dec_in, in0=dec_tmp[:, 0], in1=dec_tmp[:, 1], op=ALU.add).then_inc(dec_v.sem, 1)
                w(V, dec_v, l, 1)
                for tt in range(NS):
                    w(V, z_a, l, 3 * NT + tt + 1)
                    rope(zr[:, tt, 0:2, :].rearrange("p i c -> p (i c)"), rope_tmp, rope_r, P).then_inc(rr_v.sem, 1)
                    w(V, rr_v, l, tt + 1)

                def att_out(tt):
                    w(V, pv_p, l, HQ * (tt + 1))
                    step.do(V.reciprocal(recip[:, HQ * tt:HQ * tt + HQ], psums[:, HQ * tt:HQ * tt + HQ]))
                    TT(out=zq[:, tt, 0:512].rearrange("p (h d) -> p h d", d=DH),
                       in0=bank(6 + tt % 2).rearrange("p (h d) -> p h d", d=DH),
                       in1=recip[:, HQ * tt:HQ * tt + HQ].unsqueeze(2).broadcast_to([P, HQ, DH]),
                       op=ALU.mult).then_inc(at_v.sem, 1)

                for u in range(NT * HQ):
                    w(V, s_p, l, u + 1)
                    n = 640 if u // HQ < NS else P
                    V.tensor_reduce(negmax[:, u:u + 1], two(2 * (u % 2))[:, 0:n], AX.X, ALU.max,
                                    negate=True).then_inc(mx_v.sem, 1)
                    if u >= 9 and (u - 9) % HQ == 0:
                        att_out((u - 9) // HQ)
                att_out(NT - 1)

                w(V, st_a, l, 2)
                for n, (back, tt) in enumerate(STATES):
                    w(V, kv_p, l, n + 1)
                    if tt == PROMPT:
                        V.tensor_copy(st_buf[back], bank(n % 2)).then_inc(kv_v.sem, 1)
                        continue
                    old, new = (sb_st[tt], sb_st[tt - 1]) if back else (sf_st[tt], sf_st[tt + 1])
                    step.do(TT(out=heads(st_tmp), in0=heads(old),
                               in1=dec_chunk[:, 4 * back:4 * back + 4].unsqueeze(2).broadcast_to([P, HR, P]),
                               op=ALU.mult))
                    TT(out=new, in0=st_tmp, in1=bank(n % 2), op=ALU.add).then_inc(kv_v.sem, 1)
                    w(V, kv_v, l, n + 1)
                w(V, kv_out, l, 32)
                for tt in range(NT):
                    w(V, rq_p, l, tt + 1)
                    if tt < NS:
                        step.mark(TT(out=rqTf, in0=heads(bank(2)), in1=dec_q[:, 0], op=ALU.mult))
                        step.mark(TT(out=rqTb, in0=heads(bank(2)), in1=dec_q[:, 1], op=ALU.mult))
                    V.tensor_copy(flat(rqT), bank(2)).then_inc(rq_v.sem, 1)
                    w(V, in_p, l, tt + 1)
                    TT(out=inner[tt % 2], in0=heads(bank(4)), in1=dec_in, op=ALU.mult).then_inc(in_v.sem, 1)
                    w(V, o_p, l, tt + 1)
                    for h in range(HR):
                        step.mark(V.bn_stats(bn[:, 6 * h:6 * h + 6], bank(6)[:, h * P:(h + 1) * P]))
                    step.settle()
                    for h in range(HR):
                        step.mark(V.bn_aggr(mean_var[:, 2 * h:2 * h + 2], bn[:, 6 * h:6 * h + 6]))
                    step.settle()
                    step.do(V.tensor_copy(bna[:, 0:4], mean_var[:, 1:8:2]))
                    inverse_root(bna[:, 0:4], bna[:, 4:8], 1.0)
                    for h in range(HR):
                        hs = slice(h * P, (h + 1) * P)
                        step.mark(TS(out=o_tmp[:, hs], in0=bank(6)[:, hs], scalar1=mean_var[:, 2 * h:2 * h + 1],
                                     scalar2=bna[:, 4 + h:5 + h], op0=ALU.subtract, op1=ALU.mult))
                    step.settle()
                    step.do(TT(out=o_tmp, in0=o_tmp, in1=ret_gain, op=ALU.mult))
                    w(V, gr_a, l, tt + 1)
                    TT(out=o_tmp, in0=o_tmp, in1=sgr, op=ALU.mult).then_inc(rn_v.sem, 1)
                V.tensor_copy(h_hi, hT[:, :]).then_inc(hh_v.sem, 1)

                def split_gate(n):
                    br, c = divmod(n, KD)
                    name = f"g{br}{c // 4}"
                    V.wait_ge(full[slot_of[l, name]], full_at((l, name)))
                    if n >= 3:
                        w(V, g_p, l, n - 2)
                    raw, rest = (m[slot_of[l, name]].rearrange("p (k c) -> p k c", k=KD)[:, :, (c % 4) * P:(c % 4 + 1) * P]
                                 for m in (slot, slot_r))
                    high = w_hi[n % 3].rearrange("p (k c) -> p k c", k=KD)
                    step.do(V.tensor_copy(high, raw))
                    TT(out=rest, in0=raw, in1=high.bitcast(F32), op=ALU.subtract).then_inc(wg_v.sem, 1)

                w(V, st_out, l, 32)
                for n in range(3):
                    split_gate(n)
                for tt in range(NT):
                    w(V, m_a, l, NT + tt + 1)
                    step.do(V.tensor_tensor_reduce(mlp_tmp, gv[:, tt, :], gv[:, tt, :], 1.0, 0.0, ALU.mult, ALU.add,
                                                   st[:, tt:tt + 1]))
                inverse_root(st[:, 0:NT], st2[:, 0:NT], 1.0 / 512)
                for tt in range(NT):
                    STT(out=gv[:, tt, :], in0=gv[:, tt, :], scalar=st2[:, tt:tt + 1], in1=mlp_gain, op0=ALU.mult,
                        op1=ALU.mult).then_inc(vn_v.sem, 1)
                for tt in range(NT):
                    w(V, f_p, l, tt + 1)
                    for g in range(4):
                        gs = slice(g * P, (g + 1) * P)
                        i = STT(out=cmb[tt % 2][:, gs], in0=bank(4 + tt % 2)[:, gs], scalar=bs[:, g:g + 1],
                                in1=gu[:, tt, gs], op0=ALU.add, op1=ALU.mult)
                    i.then_inc(cm_v.sem, 1)
                for n in range(24):
                    c = n % KD
                    w(V, g_a, l, n + 1)
                    w(V, o3_p, l, n + 1)
                    prod = halves(4 + 2 * (n % 2))
                    if n < KD:
                        TT(out=in_halves(mixT[:, c, :]), in0=in_halves(sg[n % 2]), in1=prod, op=ALU.mult).then_inc(mix_v.sem, 1)
                    else:
                        w(V, mix_v, l, n)
                        step.do(TT(out=in_halves(mix_tmp), in0=in_halves(sg[n % 2]), in1=prod, op=ALU.mult))
                        TT(out=mixT[:, c, :], in0=mixT[:, c, :], in1=mix_tmp, op=ALU.add).then_inc(mix_v.sem, 1)
                    if n + 3 < 24:
                        split_gate(n + 3)
                def gain_of(cond):
                    step.do(STT(out=gain2[cond], in0=gain2[cond], scalar=1.0, in1=norm2_row, op0=ALU.add,
                                op1=ALU.mult))

                def residual(tt):
                    for half in range(2):
                        cs = slice(half * 512, half * 512 + 512)
                        q = 2 * tt + half
                        w(V, w_p, l, q + 1)
                        if q >= 1:
                            w(V, x_v, l, q)
                        step.do(TT(out=out_tmp, in0=bank(q % 4), in1=gate1[:, cond_of(tt), cs], op=ALU.mult))
                        TT(out=xh[:, tt, cs], in0=xh[:, tt, cs], in1=out_tmp, op=ALU.add).then_inc(x_v.sem, 1)

                def norm_mid(tt):
                    cond = cond_of(tt)
                    w(V, ssq2, l, tt + 1)
                    inverse_root(st[:, tt:tt + 1], st2[:, tt:tt + 1], 1.0 / D)
                    step.do(STT(out=h2[:, tt, :], in0=xh[:, tt, :], scalar=st2[:, tt:tt + 1], in1=gain2[cond],
                                op0=ALU.mult, op1=ALU.mult))
                    TT(out=h2[:, tt, :], in0=h2[:, tt, :], in1=shift2[cond], op=ALU.add).then_inc(h2_v.sem, 1)

                def take_h2(tt):
                    w(V, h2_p, l, tt + 1)
                    V.tensor_copy(h2T[:, 4:8, tok(tt)], heads(bank(5 + 2 * (tt % 2)))).then_inc(h2_q.sem, 1)

                w(V, mod2_in, l, 48)
                gain_of(0)
                w(V, res_in, l, 48)
                for tt in range(NT):
                    residual(tt)
                    if tt == PROMPT:
                        w(V, mod2p_in, l, 32)
                        gain_of(1)
                    norm_mid(tt)
                    if tt >= 1:
                        take_h2(tt - 1)
                take_h2(NT - 1)

                def tiles_of(ap):
                    return ap.unsqueeze(1).broadcast_to([P, NT, NE])

                def per_tile(ap):
                    return ap.unsqueeze(2).broadcast_to([P, NT, NE])

                def dot(out, a, b):
                    step.do(TT(out=r_tmp, in0=a, in1=b, op=ALU.mult))
                    step.do(V.tensor_reduce(out, r_tmp, AX.X, ALU.add))

                w(V, sc_a, l, 1)
                V.wait_ge(const_in, 32)
                step.mark(V.memset(r_gs, -BIG))
                step.do(TT(out=r_sel, in0=r_sc, in1=tiles_of(b_rt), op=ALU.add))
                s4 = [flat(r_sel)[:, e:NT * NE:EPG] for e in range(EPG)]
                step.mark(TT(out=r_m1, in0=s4[0], in1=s4[1], op=ALU.max))
                step.mark(TT(out=r_n1, in0=s4[0], in1=s4[1], op=ALU.min))
                step.mark(TT(out=r_m2, in0=s4[2], in1=s4[3], op=ALU.max))
                step.do(TT(out=r_n2, in0=s4[2], in1=s4[3], op=ALU.min))
                step.do(TT(out=r_n1, in0=r_n1, in1=r_n2, op=ALU.max))
                step.do(TT(out=r_n2, in0=r_m1, in1=r_m2, op=ALU.min))
                step.do(TT(out=r_m1, in0=r_m1, in1=r_m2, op=ALU.max))
                step.do(TT(out=r_n1, in0=r_n1, in1=r_n2, op=ALU.max))
                step.do(TT(out=r_gs[:, :, 0:NG], in0=r_m1.rearrange("p (t g) -> p t g", g=NG),
                           in1=r_n1.rearrange("p (t g) -> p t g", g=NG), op=ALU.add))
                for tt in range(NT):
                    step.do(V.max(r_top[:, tt, :], r_gs[:, tt, :]))
                    step.mark(V.max_index(r_gi[:, tt, :], r_top[:, tt, :], r_gs[:, tt, :]))
                step.settle()
                step.do(V.tensor_copy(r_gf, r_gi[:, :, 0]))
                step.do(TT(out=r_mask, in0=tiles_of(group_e), in1=per_tile(r_gf), op=ALU.is_equal))
                step.do(TS(out=r_mask, in0=r_mask, scalar1=-1.0, scalar2=BIG, op0=ALU.add, op1=ALU.mult))
                step.do(TT(out=r_masked, in0=r_sel, in1=r_mask, op=ALU.add))
                for tt in range(NT):
                    step.do(V.max(r_top[:, tt, :], r_masked[:, tt, :]))
                    step.mark(V.max_index(r_ei[:, tt, :], r_top[:, tt, :], r_masked[:, tt, :]))
                step.settle()
                for n in range(2):
                    step.do(V.tensor_copy(r_ef[n], r_ei[:, :, n]))
                    step.do(TT(out=(r_oh0, r_oh1)[n], in0=tiles_of(iota_e), in1=per_tile(r_ef[n]), op=ALU.is_equal))
                TT(out=r_oh, in0=r_oh0, in1=r_oh1, op=ALU.add).then_inc(oh_v.sem, 1)
                for n in range(2):
                    dot(r_w[n], r_sc, (r_oh0, r_oh1)[n])
                step.do(TT(out=r_sum, in0=r_w[0], in1=r_w[1], op=ALU.add))
                step.do(V.reciprocal(r_sum, r_sum))
                for n in range(2):
                    step.mark(TT(out=r_wn[n], in0=r_w[n], in1=r_sum, op=ALU.mult))
                w(V, rk_p2, l, 1)
                step.do(V.tensor_copy(r_cnt, ps[:, 1, 80:96]))
                step.do(TS(out=r_ov, in0=r_cnt, scalar1=full_blocks[:, 0:1], scalar2=None, op0=ALU.is_gt))
                for m in range(1, NT - 1):
                    step.do(STT(out=r_ov, in0=r_cnt, scalar=full_blocks[:, m:m + 1], in1=r_ov, op0=ALU.is_gt,
                                op1=ALU.add))
                step.do(V.tensor_copy(r_c0, r_ov))
                src, dst = r_c0, r_c1
                for sft in (1, 2, 4, 8):
                    step.mark(V.tensor_copy(dst[:, 0:sft], src[:, 0:sft]))
                    step.do(TT(out=dst[:, sft:NE], in0=src[:, sft:NE], in1=src[:, 0:NE - sft], op=ALU.add))
                    src, dst = dst, src
                run = src
                step.do(TT(out=r_ex, in0=run, in1=r_ov, op=ALU.subtract))
                step.do(TS(out=r_ex, in0=r_ex, scalar1=float(NE - 1), scalar2=None, op0=ALU.add))
                for n in range(2):
                    oh = (r_oh0, r_oh1)[n]
                    dot(r_rank[n], ps[:, 1, 0:80].rearrange("p (t e) -> p t e", e=NE), oh)
                    dot(r_ob, tiles_of(r_ex), oh)
                    step.mark(TS(out=r_hi, in0=r_rank[n], scalar1=float(P), scalar2=None, op0=ALU.is_ge))
                    step.do(TS(out=r_fl, in0=r_rank[n], scalar1=float(P), scalar2=None, op0=ALU.is_ge))
                    for m in range(1, NT - 1):
                        step.do(STT(out=r_fl, in0=r_rank[n], scalar=full_blocks[:, m:m + 1], in1=r_fl, op0=ALU.is_ge,
                                    op1=ALU.add))
                    step.mark(STT(out=r_mod[n], in0=r_fl, scalar=-float(P), in1=r_rank[n], op0=ALU.mult, op1=ALU.add))
                    step.do(TT(out=r_ob, in0=r_ob, in1=r_ef[n], op=ALU.subtract))
                    step.do(TT(out=r_hi, in0=r_hi, in1=r_ob, op=ALU.mult))
                    step.do(TT(out=r_hi, in0=r_hi, in1=r_ef[n], op=ALU.add))
                    step.mark(STT(out=r_dest[n], in0=r_hi, scalar=float(P), in1=r_rank[n], op0=ALU.mult, op1=ALU.add))
                    step.do(TT(out=r_fl, in0=r_hi, in1=r_fl, op=ALU.add))
                    step.do(TT(out=block_oh[n], in0=iota_b.unsqueeze(1).broadcast_to([P, NT, NTAB]),
                               in1=r_fl.unsqueeze(2).broadcast_to([P, NT, NTAB]), op=ALU.is_equal))
                    step.do(TT(out=block_oh[n], in0=block_oh[n], in1=token_id.unsqueeze(2).broadcast_to([P, NT, NTAB]),
                               op=ALU.mult))
                    TT(out=slot_oh[n], in0=iota_s.unsqueeze(1).broadcast_to([P, NT, P]),
                       in1=r_mod[n].unsqueeze(2).broadcast_to([P, NT, P]), op=ALU.is_equal).then_inc(tab_v.sem, 1)
                for n in range(2):
                    step.do(V.tensor_copy(slots_u[:, DEST + NT * n:DEST + NT * n + NT], r_dest[n]))
                step.mark(V.tensor_copy(slots_u[:, N_OVER:N_OVER + 1], run[:, NE - 1:NE]))
                step.do(TT(out=r_le, in0=run.unsqueeze(1).broadcast_to([P, OVER, NE]),
                           in1=iota_b[:, 0:OVER].unsqueeze(2).broadcast_to([P, OVER, NE]), op=ALU.is_le))
                step.do(V.tensor_reduce(r_eo, r_le, AX.X, ALU.add))
                step.do(TS(out=r_eo, in0=r_eo, scalar1=float(NE - 1), scalar2=None, op0=ALU.min))
                V.tensor_copy(slots_u[:, E_OVER:E_OVER + OVER], r_eo).then_inc(de_v.sem, 1)
                w(V, tk_p, l, 1)
                V.tensor_copy(slots_u[:, 0:NTAB], ps[:, 2, 0:NTAB]).then_inc(tk_v.sem, 1)
                w(V, de_v, l, 1)
                w(V, tk_v, l, 1)
                if l + 1 < LAYERS:
                    V.wait_ge(mod_st, 16 * (2 * l + 3))

                def pair(j, n0):
                    for b in range(2):
                        V.wait_ge(si_a.sem, si_a.at(l, n0 + b + 1) + 2 * j)
                        V.wait_ge(a_p.sem, a_p.at(l, 2 * (n0 + b) + 2) + 4 * j)
                        TT(out=hd[b], in0=sa[b], in1=bank(4 + b), op=ALU.mult).then_inc(hd_v.sem, 1)
                        V.wait_ge(ht_p.sem, ht_p.at(l, n0 + b + 1) + 2 * j)
                        V.tensor_copy(hdT[b], bank(6)).then_inc(ht_v.sem, 1)

                with V.Fori(0, PAIRS) as j:
                    pair(j, 0)
                n_over = V.value_load(slots_u[0:1, N_OVER:N_OVER + 1], min_val=0, max_val=9)
                w(V, hd_v, l, NE)
                w(V, ht_v, l, NE)
                with V.If(n_over > 0):
                    with V.Fori(0, OVER_PAIRS) as j:
                        pair(j, NE)
                with V.Else():
                    V.sem_inc(hd_v.sem, OVER)
                    V.sem_inc(ht_v.sem, OVER)
                w(V, g2_in, l, 32)
                w(V, y_p, l, 2 * NB2)
                for tt in range(NT):
                    b = tt % 2
                    w(V, w0_a, l, tt + 1)
                    w(V, y2_in[b], l, 16 * (tt // 2 + 1))
                    step.do(STT(out=y1[b], in0=y2[b], scalar=r_wn[1][:, tt:tt + 1], in1=y1[b], op0=ALU.mult,
                                op1=ALU.add))
                    step.do(TT(out=y1[b], in0=y1[b], in1=gate2[:, cond_of(tt), :], op=ALU.mult))
                    TT(out=xr[:, tt, :], in0=xh[:, tt, :], in1=y1[b], op=ALU.add).then_inc(cb_v.sem, 1)
                    if l + 1 < LAYERS and tt >= 1:
                        norm_in(l + 1, tt - 1)
                if l + 1 < LAYERS:
                    norm_in(l + 1, NT - 1)
                    w(V, cb_v, l, NT)

        @block.gpsimd
        def _(pool):
            G = pool
            def load_bias(batch, l):
                base, first = mod_batch[batch]
                n = (MODT, MOD_A, MODT - MOD_A)[batch] * 512
                G.dma_start(work[64:65, base:base + n], I["b_mod"][l:l + 1, first * 512:first * 512 + n]
                            ).then_inc(bias_in, 16)

            def store_mods(batch, l, t0, t1):
                base, first = mod_batch[batch]
                G.wait_ge(mod_ev, l * MODT + t1)
                G.dma_start(mod_dram[l].rearrange("s m d -> s (m d)")[:, t0 * 512:t1 * 512],
                            work[0:2, base + (t0 - first) * 512:base + (t1 - first) * 512]).then_inc(mod_st, 16)

            def spread(out, ap):
                return G.dma_start(out, ap.partition_broadcast(P))

            def layer_inputs(l):
                G.dma_start(mod_rows[32:40, :], I["norm1"][l].rearrange("(k p) -> k p", p=P)).then_inc(aux_in.sem, 16)
                for out, nm in ((qk_gain[:, 0:DH], "q_norm"), (qk_gain[:, DH:2 * DH], "k_norm"),
                                (ret_gain, "ret_gn"), (mlp_gain, "mlp_norm"), (lg[:, 0:4], "ret_decay_fwd"),
                                (lg[:, 4:8], "ret_decay_bwd")):
                    spread(out, I[nm][l]).then_inc(aux_in.sem, 16)
                G.dma_start(ws_raw.rearrange("p (g j) -> p g j", g=4),
                            I["w_spatial"][l].rearrange("g i j -> i g j")).then_inc(aux_in.sem, 16)
                with nc.allow_non_contiguous_dma(reason="512 numbers, once per layer"):
                    G.dma_start(bs, I["b_spatial"][l].rearrange("g i -> i g")).then_inc(aux_in.sem, 16)
                G.dma_start(kc_raw, I["cache_k"][:, l].rearrange("b t h d -> (b t) (h d)")).then_inc(aux_in.sem, 16)
                G.dma_start(v_cache, I["cache_v"][:, l].rearrange("b t h d -> (b t) (h d)")).then_inc(aux_in.sem, 16)
                for n, nm in enumerate(("state_ret_fwd", "state_ret_bwd")):
                    G.dma_start(heads(s_raw[:, 512 * n:512 * n + 512]),
                                I[nm][:, l].rearrange("b h d e -> d (b h) e")).then_inc(aux_in.sem, 16)
                G.dma_start(dist, I["distances"]).then_inc(aux_in.sem, 16)

            def first_mod_rows(l):
                for cond in range(2):
                    G.dma_start(mod_rows[2 * KD * cond:2 * KD * cond + 2 * KD, :],
                                mod_dram[l, cond, 0:2, :].rearrange("m (k p) -> (m k) p", p=P)
                                ).then_inc(modr_in.sem, 16)

            load_bias(0, 0)
            G.wait_ge(full[1], 16)
            G.dma_start(xr[:, 0:NS, :], I["x_sample"].rearrange("o (t p) d -> p (o t) d", p=P)).then_inc(xin, 16)
            G.dma_start(xr[:, PROMPT, :], I["x_prompt"].rearrange("o p d -> (o p) d")).then_inc(xin, 16)
            G.dma_start(w_rt.rearrange("p (k e) -> p k e", k=KD),
                        I["w_router"].rearrange("(k p) e -> p k e", p=P)).then_inc(const_in, 16)
            G.dma_start(b_rt, I["b_router"].partition_broadcast(P)).then_inc(const_in, 16)
            layer_inputs(0)
            store_mods(0, 0, 0, 4)
            G.wait_ge(mod_st, 16)
            first_mod_rows(0)
            store_mods(0, 0, 4, MODT)

            for l in range(LAYERS):
                def mod_row_of(cond, m):
                    return mod_dram[l, cond, m, :]

                if l == 0:
                    G.wait_ge(xin, 32)
                else:
                    w(G, cb_v, l - 1, NT)
                G.dma_start(x_dram.rearrange("(t p) d -> p t d", p=P), xr).then_inc(xs_out.sem, 16)
                for n, name in enumerate(("qr", "kr", "vr")):
                    s_ = slot_of[l, name]
                    w(G, zh_v, l, n + 1)
                    G.tensor_tensor(out=slot_r[s_], in0=slot[s_], in1=slot_r[high_slot[name]].bitcast(F32),
                                    op=ALU.subtract).then_inc(zl_g.sem, 1)
                w(G, qk_v, l, NT)
                w(G, z_a, l, 2 * NT)
                for n, nm in enumerate(("new_k", "new_v")):
                    G.dma_start(O[nm][:, l].rearrange("b t h d -> (b t) (h d)"),
                                zq[:, PROMPT, 512 + P * n:640 + P * n]).then_inc(kv_out.sem, 16)
                w(G, z_p, l, 5 * NT)
                for n in range(2):
                    part = slice(4 * T * n, 4 * T * (n + 1))
                    G.tensor_tensor(out=hT[:, part], in0=h_high[n].bitcast(F32), in1=h_lo[:, part].bitcast(F32),
                                    op=ALU.add).then_inc(hr_g.sem, 1)
                if l == 0:
                    w(G, hr_g, l, 2)
                    G.memset(zeros, 0.0).then_inc(zeroed, 1)
                    G.wait_ge(zeroed, 1)
                    for half in range(2):
                        G.dma_start(y_dram[NE * P:NBLK * P, half * 512:half * 512 + 512].rearrange("(b p) d -> p b d", p=P),
                                    zeros.unsqueeze(1).broadcast_to([P, OVER, 512])).then_inc(y_zero, 16)
                w(G, rr_v, l, NS)
                w(G, z_a, l, 5 * NT)
                w(G, dec_a, l, 1)
                w(G, s_p, l, NT * HQ)
                w(G, qt_a, l, NT + 1)
                for n, (back, tt) in enumerate(STATES):
                    if n >= 2:
                        w(G, kv_p, l, n - 1)
                    G.tensor_tensor(out=heads(kdec[n % 2]), in0=heads(zr[:, tt, 1, :]),
                                    in1=dec_k[:, 4 * back:4 * back + 4].unsqueeze(2).broadcast_to([P, HR, P]),
                                    op=ALU.mult).then_inc(kd_g.sem, 1)
                for back, nm in enumerate(("new_sf", "new_sb")):
                    w(G, kv_v, l, 7 + back)
                    G.dma_start(O[nm][:, l].rearrange("b h d e -> d (b h) e"),
                                heads(st_buf[back])).then_inc(st_out.sem, 16)
                w(G, hh_v, l, 1)
                w(G, m_p, l, 2 * NT)
                for n in range(2):
                    part = slice(n * 4 * T, (n + 1) * 4 * T)
                    G.tensor_tensor(out=h_lo[:, part], in0=hT[:, part], in1=h_hi[:, part].bitcast(F32),
                                    op=ALU.subtract
                                    ).then_inc(hl_g.sem, 1)
                w(G, xs_out, l, 16)
                G.wait_ge(mod_st, 32 * (l + 1))
                w(G, cm_v, l, NT)
                for cond in range(2):
                    spread(gate1[:, cond, :], mod_row_of(cond, 2)).then_inc(res_in.sem, 16)
                w(G, g_p, l, 24)
                spread(shift2[0], mod_row_of(0, 3)).then_inc(mod2_in.sem, 16)
                spread(gain2[0], mod_row_of(0, 4)).then_inc(mod2_in.sem, 16)
                spread(norm2_row, I["norm2"][l]).then_inc(mod2_in.sem, 16)
                G.dma_start(xh, x_dram.rearrange("(t p) d -> p t d", p=P)).then_inc(res_in.sem, 16)
                w(G, o3_p, l, 24)
                spread(shift2[1], mod_row_of(1, 3)).then_inc(mod2p_in.sem, 16)
                spread(gain2[1], mod_row_of(1, 4)).then_inc(mod2p_in.sem, 16)
                for tt in range(NT):
                    w(G, h2_v, l, tt + 1)
                    G.dma_start(h2_dram[tok(tt), :], h2[:, tt, :]).then_inc(h2_out.sem, 16)
                if l + 1 < LAYERS:
                    w(G, ssq2, l, NT)
                    load_bias(1, l + 1)
                w(G, lo_p, l, 1)
                for cond in range(2):
                    spread(gate2[:, cond, :], mod_row_of(cond, 5)).then_inc(g2_in.sem, 16)
                if l + 1 < LAYERS:
                    layer_inputs(l + 1)
                w(G, de_v, l, 1)
                w(G, tk_v, l, 1)
                w(G, h2_out, l, 16 * NT)

                def gather(b, col):
                    G.tensor_copy(slots_u[:, BLK_IDX + b:BLK_IDX + b + 1], slots_u[:, col]).then_inc(idx_g.sem, 1)

                def fetch(b):
                    G.indirect_dma_start(xb[b], None, h2_dram,
                                         bass.IndirectOffsetOnAxis(ap=slots_u[:, BLK_IDX + b:BLK_IDX + b + 1], axis=0)
                                         ).then_inc(xb_in[b].sem, 16)

                gather(0, slice(0, 1))
                w(G, idx_g, l, 1)
                fetch(0)
                if l + 1 < LAYERS:
                    store_mods(1, l + 1, 0, MOD_A)
                    G.wait_ge(mod_st, 16 * (2 * l + 3))
                    first_mod_rows(l + 1)

                def pair(j, n0):
                    w_loop(G, xt_p, xt_p.at(l, n0 + 1) + 2 * j)
                    for b, n in ((1, n0 + 1), (0, n0 + 2)):
                        gather(b, bass.ds(2 * j + n, 1))
                        w_loop(G, idx_g, idx_g.at(l, n + 1) + 2 * j)
                        fetch(b)

                with G.Fori(0, PAIRS) as j:
                    pair(j, 0)
                n_over = G.value_load(slots_u[0:1, N_OVER:N_OVER + 1], min_val=0, max_val=9)
                w(G, idx_g, l, NE + 1)
                w(G, xt_p, l, NE + 1)
                for b in range(2):
                    w(G, xb_in[b], l, 16 * (PAIRS + 1 - b))
                with G.If(n_over > 0):
                    with G.Fori(0, OVER_PAIRS) as j:
                        pair(j, NE)
                with G.Else():
                    G.sem_inc(idx_g.sem, OVER)
                    for b in range(2):
                        G.dma_start(xb[b][0:16, 0:16], h2_dram[0:16, 0:16]).then_inc(xb_in[b].sem, 16 * OVER_PAIRS)
                for b in range(2):
                    w(G, xb_in[b], l, xb_in[b].per)
                w(G, y_p, l, 2 * NB2)
                for b in range(2):
                    w(G, y_out[b], l, y_out[b].per)
                if l + 1 < LAYERS:
                    load_bias(2, l + 1)
                G.wait_ge(y_zero, 32)
                for tt in range(NT):
                    b = tt % 2
                    if tt >= 2:
                        w(G, cb_v, l, tt - 1)
                    for n, (dst, sig) in enumerate(((y1[b], y1_in[b]), (y2[b], y2_in[b]))):
                        c = DEST + NT * n + tt
                        G.indirect_dma_start(dst, None, y_dram, bass.IndirectOffsetOnAxis(ap=slots_u[:, c:c + 1], axis=0)
                                             ).then_inc(sig.sem, 16)
                if l + 1 < LAYERS:
                    store_mods(2, l + 1, MOD_A, MODT)
                else:
                    for tt in range(NT):
                        w(G, cb_v, l, tt + 1)
                        out = O["y_sample"][0, tok(tt), :] if tt < NS else O["y_prompt"][0]
                        G.dma_start(out, xr[:, tt, :]).then_inc(fin_out, 16)
            G.wait_ge(kv_out.sem, LAYERS * kv_out.per)
            G.wait_ge(st_out.sem, LAYERS * st_out.per)
            G.wait_ge(fin_out, 16 * NT)


_INS = ["x_prompt", "x_sample", "cache_k", "cache_v", "state_ret_fwd", "state_ret_bwd", "c", "c_ctx", "w_mod", "b_mod",
        "norm1", "norm2", "w_in", "q_norm", "k_norm", "ret_decay_fwd", "ret_decay_bwd", "ret_gn", "mlp_norm",
        "w_spatial", "b_spatial", "w_att_o", "w_ret_o", "w_mlp_o", "w_out", "w_router", "b_router", "w_gate", "w_up",
        "w_down"]
_OUTS = [("y_prompt", (1, P, D)), ("y_sample", (1, NS * P, D)), ("new_k", (1, LAYERS, P, HKV, DH)),
         ("new_v", (1, LAYERS, P, HKV, DH)), ("new_sf", (1, LAYERS, HR, P, P)), ("new_sb", (1, LAYERS, HR, P, P))]


def kernel(**inputs):
    import numpy as _np
    import concourse.bacc as _bacc
    from concourse import mybir as _mybir
    from concourse.bass_utils import run_bass_kernel_spmd as _run

    nc = _bacc.Bacc("TRN2", target_bir_lowering=False, num_devices=1)
    arrays, ins, outs = {}, {}, {}
    for name in _INS:
        a = _np.ascontiguousarray(inputs[name])
        arrays[f"in_{name}_dram"] = a
    arrays["in_persistent_dram"] = PERSISTENT
    arrays["in_distances_dram"] = DISTANCES
    for key, a in arrays.items():
        ins[key[3:-5]] = nc.dram_tensor(key, a.shape, _mybir.dt.from_np(a.dtype), kind="ExternalInput").ap()
    for i, (name, shape) in enumerate(_OUTS):
        outs[name] = nc.dram_tensor(f"out_{i}_dram", shape, _mybir.dt.float32, kind="ExternalOutput").ap()
    trunk(nc, ins, outs)
    r = _run(nc, [arrays], core_ids=[0])
    return tuple(r.results[0][f"out_{i}_dram"] for i in range(len(_OUTS)))
```
